# Optimizing a Trainium2 kernel written in Bass

```python
import jax, jax.numpy as jnp
from jax import lax
import numpy as np

D_MODEL = 1024
BATCH = 1
SEQ = 256
DEPTH = 2

N_MEM = 256
RET_HEADS = 4
RET_HEAD_DIM = 128
RET_WIDTH = RET_HEADS * RET_HEAD_DIM
RET_CHUNK = 128
CONV_CH = 512
CONV_WIDTH = 31
XATTN_HEADS = 4
XATTN_HEAD_DIM = 128
XATTN_WIDTH = XATTN_HEADS * XATTN_HEAD_DIM
N_EXPERTS = 16
N_GROUPS = 4
EXPERTS_PER_GROUP = N_EXPERTS // N_GROUPS
TOP_K = 2
D_EXPERT = 512
ROPE_BASE = 10000.0
EPS = 1e-6
IN_COLS = 4 * RET_WIDTH + 2 * CONV_CH + 2 * D_MODEL

kernel_name = 'hybrid_retention_conformer_xattn_grouped_moe'

def _rmsnorm(x, g):
    xf = x.astype(jnp.float32)
    y = xf * lax.rsqrt(jnp.mean(xf * xf, axis=-1, keepdims=True) + EPS)
    return (y * g.astype(jnp.float32)).astype(x.dtype)

def _rotary(t, positions):
    half = t.shape[-1] // 2
    inv_freq = ROPE_BASE ** (-jnp.arange(half, dtype=jnp.float32) / half)
    ang = positions.astype(jnp.float32)[:, None] * inv_freq[None, :]
    cos = jnp.cos(ang)[None, :, None, :]
    sin = jnp.sin(ang)[None, :, None, :]
    tf = t.astype(jnp.float32)
    t1, t2 = tf[..., :half], tf[..., half:]
    return jnp.concatenate([t1 * cos - t2 * sin, t2 * cos + t1 * sin], axis=-1).astype(t.dtype)

def _retention(q, k, v):
    b, s, h, dh = q.shape
    c = RET_CHUNK
    n = s // c
    log_gamma = jnp.log(1.0 - 2.0 ** (-5.0 - jnp.arange(h, dtype=jnp.float32)))
    qf = q.astype(jnp.float32).reshape(b, n, c, h, dh)
    kf = k.astype(jnp.float32).reshape(b, n, c, h, dh) * (dh ** -0.5)
    vf = v.astype(jnp.float32).reshape(b, n, c, h, dh)
    idx = jnp.arange(c, dtype=jnp.float32)
    diff = idx[:, None] - idx[None, :]
    decay = jnp.where(diff[None] >= 0.0,
                      jnp.exp(jnp.maximum(diff, 0.0)[None] * log_gamma[:, None, None]), 0.0)
    scores = jnp.einsum('bnihd,bnjhd->bnhij', qf, kf) * decay[None, None]
    inner = jnp.einsum('bnhij,bnjhe->bnihe', scores, vf)
    zeta = jnp.exp((c - 1.0 - idx)[None, :] * log_gamma[:, None])
    kv = jnp.einsum('bnjhd,hj,bnjhe->nbhde', kf, zeta, vf)
    chunk_decay = jnp.exp(c * log_gamma)[None, :, None, None]

    def step(state, kv_n):
        return chunk_decay * state + kv_n, state

    _, prev = lax.scan(step, jnp.zeros((b, h, dh, dh), jnp.float32), kv)
    xi = jnp.exp((idx + 1.0)[None, :] * log_gamma[:, None])
    cross = jnp.einsum('bnihd,nbhde,hi->bnihe', qf, prev, xi)
    return (inner + cross).reshape(b, s, h, dh)

def _conv_module(u, conv_w, conv_b, ln_g, ln_b, w_proj):
    a, g = jnp.split(u, 2, axis=-1)
    z = a * jax.nn.sigmoid(g)
    z = jnp.pad(z, ((0, 0), (CONV_WIDTH - 1, 0), (0, 0)))
    z = lax.conv_general_dilated(z, conv_w[:, None, :], window_strides=(1,), padding='VALID',
                                 dimension_numbers=('NWC', 'WIO', 'NWC'),
                                 feature_group_count=CONV_CH) + conv_b
    zf = z.astype(jnp.float32)
    mu = jnp.mean(zf, axis=-1, keepdims=True)
    var = jnp.mean(jnp.square(zf - mu), axis=-1, keepdims=True)
    zf = (zf - mu) * lax.rsqrt(var + EPS) * ln_g.astype(jnp.float32) + ln_b.astype(jnp.float32)
    z = jax.nn.silu(zf).astype(u.dtype)
    return z @ w_proj

def _cross_attention(h, mem_n, w_xq, w_xkv, w_xo):
    b, s, _ = h.shape
    m = mem_n.shape[1]
    q = (h @ w_xq).reshape(b, s, XATTN_HEADS, XATTN_HEAD_DIM)
    kv = (mem_n @ w_xkv).reshape(b, m, 2, XATTN_HEADS, XATTN_HEAD_DIM)
    k, v = kv[:, :, 0], kv[:, :, 1]
    sc = jnp.einsum('bshd,bmhd->bhsm', q.astype(jnp.float32), k.astype(jnp.float32)) * (XATTN_HEAD_DIM ** -0.5)
    p = jax.nn.softmax(sc, axis=-1)
    o = jnp.einsum('bhsm,bmhd->bshd', p, v.astype(jnp.float32)).astype(h.dtype)
    return o.reshape(b, s, XATTN_WIDTH) @ w_xo

def _grouped_moe(h, w_router, b_router, w_gate, w_up, w_down):
    b, s, d = h.shape
    t = h.reshape(b * s, d)
    scores = jax.nn.sigmoid(t.astype(jnp.float32) @ w_router.astype(jnp.float32))
    sel = scores + b_router.astype(jnp.float32)
    grp = sel.reshape(-1, N_GROUPS, EXPERTS_PER_GROUP)
    grp_score = jnp.sum(lax.top_k(grp, TOP_K)[0], axis=-1)
    best_group = jnp.argmax(grp_score, axis=-1)
    in_group = (jnp.arange(N_EXPERTS) // EXPERTS_PER_GROUP)[None, :] == best_group[:, None]
    _, e_idx = lax.top_k(jnp.where(in_group, sel, -jnp.inf), TOP_K)
    w_sel = jnp.take_along_axis(scores, e_idx, axis=-1)
    w_sel = w_sel / jnp.sum(w_sel, axis=-1, keepdims=True)
    gates = jnp.sum(jax.nn.one_hot(e_idx, N_EXPERTS, dtype=jnp.float32) * w_sel[..., None], axis=1)
    y = jnp.zeros((b * s, d), jnp.float32)
    for e in range(N_EXPERTS):
        he = jax.nn.silu(t @ w_gate[e]) * (t @ w_up[e])
        y = y + gates[:, e:e + 1] * (he @ w_down[e]).astype(jnp.float32)
    return y.astype(h.dtype).reshape(b, s, d)

def setup_inputs(seed: int = 0) -> dict:
    key = jax.random.key(seed)
    ks = jax.random.split(key, 32)
    f32 = jnp.float32

    def nrm(k, shape, fan_in, scale=1.0):
        return jax.random.normal(k, shape, f32) * (scale * fan_in ** -0.5)

    def gain(k, shape):
        return 1.0 + 0.05 * jax.random.normal(k, shape, f32)

    return {
        'x': jax.random.normal(ks[0], (BATCH, SEQ, D_MODEL), f32),
        'mem': jax.random.normal(ks[1], (BATCH, N_MEM, D_MODEL), f32),
        'positions': jnp.arange(SEQ, dtype=jnp.int32),
        'norm_mix_g': gain(ks[2], (DEPTH, D_MODEL)),
        'w_in': nrm(ks[3], (DEPTH, D_MODEL, IN_COLS), D_MODEL),
        'b_branch_gate': 0.02 * jax.random.normal(ks[4], (DEPTH, 2 * D_MODEL), f32),
        'ret_norm_g': gain(ks[5], (DEPTH, RET_WIDTH)),
        'w_ret_out': nrm(ks[6], (DEPTH, RET_WIDTH, D_MODEL), RET_WIDTH),
        'conv_w': nrm(ks[7], (DEPTH, CONV_WIDTH, CONV_CH), CONV_WIDTH),
        'conv_b': 0.02 * jax.random.normal(ks[8], (DEPTH, CONV_CH), f32),
        'conv_ln_g': gain(ks[9], (DEPTH, CONV_CH)),
        'conv_ln_b': 0.02 * jax.random.normal(ks[10], (DEPTH, CONV_CH), f32),
        'w_conv_out': nrm(ks[11], (DEPTH, CONV_CH, D_MODEL), CONV_CH),
        'w_mix_out': nrm(ks[12], (DEPTH, D_MODEL, D_MODEL), D_MODEL, 0.5),
        'norm_xattn_g': gain(ks[13], (DEPTH, D_MODEL)),
        'norm_mem_g': gain(ks[14], (DEPTH, D_MODEL)),
        'w_xq': nrm(ks[15], (DEPTH, D_MODEL, XATTN_WIDTH), D_MODEL),
        'w_xkv': nrm(ks[16], (DEPTH, D_MODEL, 2 * XATTN_WIDTH), D_MODEL),
        'w_xo': nrm(ks[17], (DEPTH, XATTN_WIDTH, D_MODEL), XATTN_WIDTH, 0.5),
        'norm_ffn_g': gain(ks[18], (DEPTH, D_MODEL)),
        'w_router': nrm(ks[19], (D_MODEL, N_EXPERTS), D_MODEL),
        'b_router': 0.01 * jax.random.normal(ks[20], (N_EXPERTS,), f32),
        'w_exp_gate': nrm(ks[21], (DEPTH, N_EXPERTS, D_MODEL, D_EXPERT), D_MODEL),
        'w_exp_up': nrm(ks[22], (DEPTH, N_EXPERTS, D_MODEL, D_EXPERT), D_MODEL),
        'w_exp_down': nrm(ks[23], (DEPTH, N_EXPERTS, D_EXPERT, D_MODEL), D_EXPERT, 0.5),
        'norm_final_g': gain(ks[24], (D_MODEL,)),
    }

def reference(x, mem, positions, norm_mix_g, w_in, b_branch_gate, ret_norm_g, w_ret_out,
              conv_w, conv_b, conv_ln_g, conv_ln_b, w_conv_out, w_mix_out,
              norm_xattn_g, norm_mem_g, w_xq, w_xkv, w_xo, norm_ffn_g,
              w_router, b_router, w_exp_gate, w_exp_up, w_exp_down, norm_final_g):
    b, s, _ = x.shape
    o_q, o_k, o_v, o_g = RET_WIDTH, 2 * RET_WIDTH, 3 * RET_WIDTH, 4 * RET_WIDTH
    o_c = o_g + 2 * CONV_CH
    for l in range(DEPTH):
        h = _rmsnorm(x, norm_mix_g[l])
        u = h @ w_in[l]
        q = _rotary(u[..., :o_q].reshape(b, s, RET_HEADS, RET_HEAD_DIM), positions)
        k = _rotary(u[..., o_q:o_k].reshape(b, s, RET_HEADS, RET_HEAD_DIM), positions)
        v = u[..., o_k:o_v].reshape(b, s, RET_HEADS, RET_HEAD_DIM)
        r = _retention(q, k, v)
        r = r * lax.rsqrt(jnp.mean(r * r, axis=-1, keepdims=True) + EPS)
        r = r.reshape(b, s, RET_WIDTH) * ret_norm_g[l].astype(jnp.float32)
        r = (jax.nn.silu(u[..., o_v:o_g].astype(jnp.float32)) * r).astype(x.dtype)
        y_ret = r @ w_ret_out[l]
        y_conv = _conv_module(u[..., o_g:o_c], conv_w[l], conv_b[l], conv_ln_g[l], conv_ln_b[l],
                              w_conv_out[l])
        gate = jax.nn.sigmoid(u[..., o_c:] + b_branch_gate[l])
        g_ret, g_conv = gate[..., :D_MODEL], gate[..., D_MODEL:]
        x = x + (g_ret * y_ret + g_conv * y_conv) @ w_mix_out[l]
        x = x + _cross_attention(_rmsnorm(x, norm_xattn_g[l]), _rmsnorm(mem, norm_mem_g[l]),
                                 w_xq[l], w_xkv[l], w_xo[l])
        x = x + _grouped_moe(_rmsnorm(x, norm_ffn_g[l]), w_router, b_router,
                             w_exp_gate[l], w_exp_up[l], w_exp_down[l])
    return _rmsnorm(x, norm_final_g)


_drawn_inputs = setup_inputs


def setup_inputs(seed=0):
    import zlib

    import numpy as np

    out = dict(_drawn_inputs(seed))
    spreads = {}
    factors = {'b_branch_gate': 3.062, 'conv_ln_b': 3.038, 'norm_mem_g': 2.825}
    for name, (base, spread) in spreads.items():
        noise = np.random.default_rng([zlib.crc32(name.encode()), seed]).standard_normal(out[name].shape)
        drawn = base * np.exp(spread * noise) if base else spread * noise
        out[name] = __import__('jax').numpy.asarray(drawn.astype(out[name].dtype))
    for name, factor in factors.items():
        out[name] = (out[name] * factor).astype(out[name].dtype)
    return out
```

```python
from contextlib import ExitStack

import numpy as np
import concourse.bass as bass
from concourse import mybir

P = 128
D = 1024
S = 256
KD = D // P
TB = S // P
HEADS = 4
CB = 4
TAPS = 31
E = 16
SLOTS = 64
PAIRS = E // 2
RING = 6
UNIT = 4096
DENSE_UNITS = 18
JOBS = 42
RB = 4
JOBS_OF_BANK = [len(range(b, JOBS, RB)) for b in range(RB)]
ZW = S + TAPS - 1
EPS = 1e-6
SCALE = float(P) ** -0.5
BIG = 1e30
TWO_PI = 2.0 * np.pi
PI_A = 6.28125
PI_B = float(np.float32(np.floor((TWO_PI - PI_A) * 2.0 ** 20) / 2.0 ** 20))
PI_C = float(TWO_PI - PI_A - PI_B)
MAGIC = 12582912.0

C_ID, C_ONE, C_SWAP, C_BEFORE = 0, 128, 256, 384
C_DECAY = 512
C_IOTA = C_DECAY + HEADS * S
C_KEY4 = C_IOTA + S
C_KEY16 = C_KEY4 + 4
C_FREQ = C_KEY16 + 16
C_EPS = C_FREQ + 1
C_ALL = C_EPS + 1

V_MIX, V_XATTN, V_MEM, V_FFN = 0, 8, 16, 24
V_BG = 32
V_RET = 48
V_CB, V_LG, V_LB = 52, 56, 60
V_TAP = 64
V_ALL = V_TAP + TAPS * CB

G_RT, G_BR, G_FIN = 0, 128, 144
G_ALL = 152

F32 = mybir.dt.float32
I32 = mybir.dt.int32
ALU = mybir.AluOpType
ACT = mybir.ActivationFunctionType
AX = mybir.AxisListType.X

DVE_LINKS = 72
PAIR_LINKS = 0

(U_CG, U_CA, U_Q, U_K, U_V, U_SG, U_G0, U_G1, U_G2, U_G3, U_XK, U_XV, U_RET, U_CONV, U_M0, U_M1, U_XQ,
 U_XO) = range(DENSE_UNITS)
LAST_JOB = [1, 3, 5, 7, 9, 11, 13, 15, 17, 19, 21, 23, 27, 31, 33, 35, 37, 41]
J_CG, J_CA, J_Q, J_K, J_V, J_SG, J_G, J_XK, J_XV, J_RET, J_CONV, J_MIX, J_XQ, J_XO = (
    0, 2, 4, 6, 8, 10, 12, 20, 22, 24, 28, 32, 36, 38)


def build(nc, xT_d, memT_d, pos_d, const_d, vec_d, glob_d, dense_d, experts_d, out_d):
    depth = dense_d.shape[0]
    ctx = ExitStack()
    with ctx:
        def sb(name, cols, dt=F32, rows=P):
            return ctx.enter_context(nc.sbuf_tensor(name, [rows, cols], dt))

        def sem(name):
            return ctx.enter_context(nc.semaphore(name))

        ring = sb("ring", RING * UNIT)
        const = sb("const", C_ALL)
        vec = sb("vec", 2 * V_ALL)
        glob = sb("glob", G_ALL)
        sin2 = sb("sin2", 2 * S)
        cos2 = sb("cos2", 2 * S)
        xT = sb("xT", KD * S)
        hT = sb("hT", KD * S)
        memhat = sb("memhat", KD * S)
        memn = sb("memn", KD * S)
        kx = sb("kx", HEADS * S)
        vx = sb("vx", TB * 512)
        gates = sb("gates", 16 * S)
        qk = sb("qk", 2 * HEADS * S)
        v = sb("v", TB * 512)
        sg = sb("sg", HEADS * S)
        zp = sb("zp", CB * (S + TAPS - 1))
        cz = sb("cz", CB * S)
        r = sb("r", HEADS * S)
        tmp = sb("tmp", KD * S)
        rstd = sb("rstd", 2 * S * 2)
        small = sb("small", 512)
        count = sb("count", 1, I32, 1)
        pos_i = tmp[:, 0:S].bitcast(I32)

        sT = memn[:, 0:HEADS * 384]
        mixin = qk
        qx = sg
        probs = gates[:, 0:2048]
        pT = gates[:, 2048:4096]
        oT = r
        tok = gates[:, 0:2048]
        onehot = gates[:, 2048:2304]
        gated = gates[:, 2304:2560]
        gatedT = gates[:, 2560:2816]
        xg = gates[:, 2816:3840]
        sig = v[:, 0:512]
        he = v[:, 512:1024]
        ye = r

        ps = [ctx.enter_context(nc.psum_tensor(f"bank{i}", [P, 512], F32)) for i in range(8)]
        R, M = ps[0:4], ps[4:8]
        GA, GU, DN, SC = ps[0:2], ps[2:4], ps[4:6], ps[6:8]

        ident = const[:, C_ID:C_ID + P]
        ones = const[:, C_ONE:C_ONE + P]
        swap = const[:, C_SWAP:C_SWAP + P]
        before = const[:, C_BEFORE:C_BEFORE + P]
        eps = const[:, C_EPS:C_EPS + 1]

        names = """const_in x_in mem_in pos_in out_sent
            start squares norm_sum norm_root normed mem_ready mem_sum mem_root
            proj_done sig_cg z_ready qk_raw swapped rotated v_ready sig_sg silu_g gate_ready
            scores masked r_sum r_copied r_squares r_norm_sum r_root ret_ready
            conv_tap conv_out ln_mean ln_squares ln_var ln_root ln_scaled ln_sig conv_ready kv_ready
            mix_ready x_mixed qx_ready att_scores att_max att_exp att_probs att_T att_pT att_o att_oT x_attended
            tok_T tok_ready logits router_sig chosen ranks sweeps_known ranks_ready
            onehot_ready gathered xg_ready gatedT_psum gatedT_ready gu_done up_sig he_ready down_done
            y_copied scattered added pair_done
            link pair_link start_link angle sin_done finished expert_used mem_squares memn_ready
            count_due""".split()
        s = {n: sem(n) for n in names}
        landed = [sem(f"weights_landed{i}") for i in range(RING)]
        bank_free = [sem(f"bank_free{i}") for i in range(RB)]

        block = ctx.enter_context(nc.Block())

        at = [0]

        def part_of_small(n):
            at[0] += n
            return small[:, at[0] - n:at[0]]

        chosen, score, gate, place = (part_of_small(TB * E) for _ in range(4))
        sel, keyed, hot2 = (part_of_small(E) for _ in range(3))
        sums, group, ingroup, best = part_of_small(24), part_of_small(4), part_of_small(4), part_of_small(1)
        neg_max, exp_sum = part_of_small(8), part_of_small(8)

        def vcol(eng, l, col):
            return vec[:, bass.ds(l * V_ALL + col, 1)]

        def slot(u):
            return ring[:, (u % RING) * UNIT:(u % RING + 1) * UNIT]

        def iterations(eng, l):
            eng.wait_ge(s["sweeps_known"], l + 1)
            eng.sem_inc(s["count_due"], 1)
            return eng.value_load(count[0:1, 0:1], min_val=PAIRS, max_val=PAIRS * (S // SLOTS))

        @block.sync
        def _(sp):
            sp.dma_start(const[:], const_d).then_inc(s["const_in"], 16)
            sp.dma_start(glob[:], glob_d).then_inc(s["const_in"], 16)
            sp.dma_start(vec[:], vec_d).then_inc(s["const_in"], 16)
            sp.dma_start(pos_i, pos_d).then_inc(s["pos_in"], 16)
            sp.dma_start(xT[:].rearrange("p (k t) -> p k t", k=KD), xT_d).then_inc(s["x_in"], 16)
            sp.dma_start(hT[:].rearrange("p (k t) -> p k t", k=KD), memT_d).then_inc(s["mem_in"], 16)
            sp.sem_inc(s["expert_used"], RING)
            pairs_done = sp.alloc_register("pairs_done")
            sp.reg_mov(pairs_done, 0)
            with sp.Fori(0, depth) as l:
                pairs = sp.snap(pairs_done)
                for u in range(DENSE_UNITS):
                    if u < RING:
                        sp.wait_ge(s["expert_used"], pairs * RING + u + 1)
                    else:
                        sp.wait_ge(s["proj_done"], l * JOBS + LAST_JOB[u - RING] + 1)
                    sp.dma_start(slot(u), dense_d[bass.ds(l, 1), u].rearrange("o p n -> p (o n)")
                                 ).then_inc(landed[u % RING], 16)
                for b in range(RING):
                    sp.wait_ge(s["proj_done"], l * JOBS + LAST_JOB[DENSE_UNITS - RING + b] + 1)
                    sp.dma_start(slot(b), experts_d[bass.ds(l * PAIRS, 1), b].rearrange("o p n -> p (o n)")
                                 ).then_inc(landed[b], 16)
                n = iterations(sp, l)
                with sp.Fori(1, n) as it:
                    t = sp.snap(pairs + it)
                    for b in range(RING):
                        sp.wait_ge(s["expert_used"], t * RING + b + 1)
                        sp.dma_start(slot(b), experts_d[bass.ds(l * PAIRS + it % PAIRS, 1), b]
                                     .rearrange("o p n -> p (o n)")).then_inc(landed[b], 16)
                sp.reg_add(pairs_done, pairs_done, n)
            sp.wait_ge(s["finished"], 1)
            sp.dma_start(out_d, hT[:].rearrange("p (k t) -> p k t", k=KD)).then_inc(s["out_sent"], 16)
            sp.wait_ge(s["out_sent"], 16)

        @block.tensor
        def _(pe):
            mm = nc.tensor.matmul

            def column_sum(out, squares, blocks):
                for k in range(blocks):
                    m = mm(out, ones, squares[:, k * S:(k + 1) * S], start=k == 0, stop=k == blocks - 1)
                return m

            pe.wait_ge(s["const_in"], 48)
            pe.wait_ge(s["mem_squares"], 1)
            column_sum(M[2][:, 0:S], tmp, KD).then_inc(s["mem_sum"], 1)
            pairs_done = pe.alloc_register("pairs_done")
            pe.reg_mov(pairs_done, 0)
            with pe.Fori(0, depth) as l:
                rounds = pe.snap(l * (DENSE_UNITS // RING) + pe.snap(pairs_done))

                def weights(u):
                    pe.wait_ge(landed[u % RING], (rounds + u // RING + 1) * 16)
                    return slot(u)

                def bank(j):
                    if j >= RB:
                        pe.wait_ge(bank_free[j % RB], l * JOBS_OF_BANK[j % RB] + j // RB)
                    return R[j % RB]

                def project(u, j, src, cols, blocks, first=True, last=True, k0=0, kn=KD):
                    w = weights(u)
                    for c in range(blocks):
                        out = bank(j + c // 2) if c % 2 == 0 else R[(j + c // 2) % RB]
                        for k in range(kn):
                            m = mm(out[:, (c % 2) * S:(c % 2 + 1) * S], w[:, k * cols + c * P:k * cols + c * P + P],
                                   src[:, k * S:(k + 1) * S], start=k == 0, stop=k == kn - 1)
                        if c % 2 == 1:
                            m.then_inc(s["proj_done"], 1)

                def project_values(u, j, src):
                    w = weights(u)
                    for b in range(TB):
                        out = bank(j + b)
                        for k in range(KD):
                            m = mm(out[:], src[:, k * S + b * P:k * S + b * P + P], w[:, k * 512:(k + 1) * 512],
                                   start=k == 0, stop=k == KD - 1)
                        m.then_inc(s["proj_done"], 1)

                pe.wait_ge(s["squares"], l * 3 + 1)
                column_sum(M[2][:, 0:S], tmp, KD).then_inc(s["norm_sum"], 1)
                pe.wait_ge(s["normed"], l * 3 + 1)
                for u, j in ((U_CG, J_CG), (U_CA, J_CA), (U_Q, J_Q), (U_K, J_K)):
                    project(u, j, hT, 512, 4)
                project_values(U_V, J_V, hT)
                for i in range(4):
                    pe.wait_ge(s["qk_raw"], l * 4 + i + 1)
                    mm(M[i][:], swap, qk[:, i * 512:(i + 1) * 512], start=True, stop=True).then_inc(s["swapped"], 1)
                project(U_SG, J_SG, hT, 512, 4)
                project(U_G0, J_G, hT, 512, 4)
                for h in range(HEADS):
                    pe.wait_ge(s["rotated"], l * 4 + 4)
                    q = qk[:, h * S:(h + 1) * S]
                    k = qk[:, (HEADS + h) * S:(HEADS + h + 1) * S]
                    mm(M[h][:, 0:S], k[:, 0:P], q, start=True, stop=True)
                    mm(M[h][:, S:S + P], k[:, P:S], q[:, P:S], start=True, stop=True).then_inc(s["scores"], 1)
                project(U_G1, J_G + 2, hT, 512, 4)
                for h in range(HEADS):
                    pe.wait_ge(s["masked"], l * HEADS + HEADS)
                    for j in (J_V, J_V + 1):
                        pe.wait_ge(bank_free[j % RB], l * JOBS_OF_BANK[j % RB] + j // RB + 1)
                    out = M[h // 2][:, (h % 2) * S:(h % 2 + 1) * S]
                    mm(out, v[:, h * P:(h + 1) * P], sT[:, h * 384:h * 384 + S], start=True, stop=False)
                    mm(out[:, P:S], v[:, 512 + h * P:512 + (h + 1) * P], sT[:, h * 384 + S:h * 384 + 384],
                       start=False, stop=True).then_inc(s["r_sum"], 1)
                project(U_G2, J_G + 4, hT, 512, 4)
                pe.wait_ge(s["r_squares"], l + 1)
                for i in range(2):
                    mm(M[2 + i][:], ones, tmp[:, i * 512:(i + 1) * 512], start=True, stop=True).then_inc(s["r_norm_sum"], 1)
                project(U_G3, J_G + 6, hT, 512, 4)
                pe.wait_ge(s["conv_tap"], (l + 1) * (TAPS * CB))
                pe.wait_ge(s["r_copied"], l + 1)
                column_sum(M[0][:, 0:S], cz, CB).then_inc(s["ln_mean"], 1)
                pe.wait_ge(s["memn_ready"], l + 1)
                project(U_XK, J_XK, memn, 512, 4)
                pe.wait_ge(s["ln_squares"], l + 1)
                column_sum(M[1][:, 0:S], tmp, CB).then_inc(s["ln_var"], 1)
                project_values(U_XV, J_XV, memn)
                pe.wait_ge(s["ret_ready"], l + 1)
                project(U_RET, J_RET, r, D, KD, kn=CB)
                pe.wait_ge(s["conv_ready"], l + 1)
                project(U_CONV, J_CONV, cz, D, KD, kn=CB)
                pe.wait_ge(s["mix_ready"], l + 1)
                for i in range(2):
                    project(U_M0 + i, J_MIX + 2 * i, mixin, 512, 4)

                pe.wait_ge(s["squares"], l * 3 + 2)
                column_sum(M[2][:, 0:S], tmp, KD).then_inc(s["norm_sum"], 1)
                pe.wait_ge(s["normed"], l * 3 + 2)
                project(U_XQ, J_XQ, hT, 512, 4)
                for j in (J_XK, J_XK + 1, J_XV, J_XV + 1, J_XQ, J_XQ + 1):
                    pe.wait_ge(bank_free[j % RB], l * JOBS_OF_BANK[j % RB] + j // RB + 1)
                for h in range(HEADS):
                    for b in range(TB):
                        m = mm(M[h][:, b * S:(b + 1) * S], qx[:, h * S + b * P:h * S + b * P + P],
                               kx[:, h * S:(h + 1) * S], start=True, stop=True)
                    m.then_inc(s["att_scores"], 1)
                for h in range(HEADS):
                    pe.wait_ge(s["att_probs"], l * HEADS + h + 1)
                    for c in range(TB):
                        for b in range(TB):
                            m = nc.tensor.transpose(M[h][:, c * S + b * P:c * S + b * P + P],
                                                    probs[:, (h * TB + b) * S + c * P:(h * TB + b) * S + c * P + P], ident)
                    m.then_inc(s["att_T"], 1)
                for h in range(HEADS):
                    pe.wait_ge(s["att_pT"], l * HEADS + HEADS)
                    for c in range(TB):
                        m = mm(M[h // 2][:, (h % 2) * S:(h % 2 + 1) * S], vx[:, c * 512 + h * P:c * 512 + (h + 1) * P],
                               pT[:, (h * TB + c) * S:(h * TB + c + 1) * S], start=c == 0, stop=c == TB - 1)
                    m.then_inc(s["att_o"], 1)
                pe.wait_ge(s["att_oT"], l * 2 + 2)
                project(U_XO, J_XO, oT, D, KD, kn=CB)

                pe.wait_ge(s["squares"], l * 3 + 3)
                column_sum(M[2][:, 0:S], tmp, KD).then_inc(s["norm_sum"], 1)
                pe.wait_ge(s["normed"], l * 3 + 3)
                for b in range(TB):
                    for k in range(KD):
                        m = mm(R[0][:, b * E:(b + 1) * E], hT[:, k * S + b * P:k * S + b * P + P],
                               glob[:, G_RT + k * E:G_RT + (k + 1) * E], start=k == 0, stop=k == KD - 1)
                m.then_inc(s["logits"], 1)
                for i in range(4):
                    for q in range(4):
                        b, k = divmod(i * 4 + q, KD)
                        m = nc.tensor.transpose(M[i][:, q * P:(q + 1) * P], hT[:, k * S + b * P:k * S + b * P + P], ident)
                    m.then_inc(s["tok_T"], 1)
                pe.wait_ge(s["chosen"], l + 1)
                ch = chosen
                mm(R[1][:, 0:E], before, ch[:, 0:E], start=True, stop=True)
                mm(R[1][:, E:2 * E], before, ch[:, E:2 * E], start=True, stop=False)
                mm(R[1][:, E:2 * E], ones, ch[:, 0:E], start=False, stop=True)
                mm(R[1][:, 2 * E:3 * E], ones, ch[:, 0:E], start=True, stop=False)
                mm(R[1][:, 2 * E:3 * E], ones, ch[:, E:2 * E], start=False, stop=True).then_inc(s["ranks"], 1)

                n = iterations(pe, l)
                with pe.Fori(0, n) as it:
                    t = pe.snap(it + pe.snap(pairs_done))
                    dense_rounds = pe.snap((l + 1) * (DENSE_UNITS // RING) + t)

                    def expert_weights(b):
                        pe.wait_ge(landed[b], (dense_rounds + 1) * 16)
                        return slot(b)

                    pe.wait_ge(s["tok_ready"], l * 4 + 4)
                    pe.wait_ge(s["onehot_ready"], t + 1)
                    for k in range(KD):
                        for b in range(TB):
                            m = mm(GA[k // 4][:, (k % 4) * P:(k % 4 + 1) * P], tok[:, b * D + k * P:b * D + (k + 1) * P],
                                   onehot[:, b * P:(b + 1) * P], start=b == 0, stop=b == TB - 1)
                        if k % 4 == 3:
                            m.then_inc(s["gathered"], 1)
                    for b in range(TB):
                        m = nc.tensor.transpose(SC[0][:, b * P:(b + 1) * P], gated[:, b * P:(b + 1) * P], ident)
                    m.then_inc(s["gatedT_psum"], 1)
                    pe.wait_ge(s["xg_ready"], t * 2 + 2)
                    for x in range(2):
                        for g in range(2):
                            w = expert_weights(2 * x + g)
                            for f in range(4):
                                for k in range(KD):
                                    m = mm(GU[x][:, (g * 4 + f) * SLOTS:(g * 4 + f + 1) * SLOTS],
                                           w[:, k * 512 + f * P:k * 512 + (f + 1) * P],
                                           xg[:, k * P + x * SLOTS:k * P + (x + 1) * SLOTS], start=k == 0, stop=k == KD - 1)
                            m.then_inc(s["expert_used"], 1)
                    for x in range(2):
                        pe.wait_ge(s["he_ready"], t * 2 + x + 1)
                        w = expert_weights(4 + x)
                        for c in range(2):
                            for f in range(4):
                                m = mm(DN[c][x * SLOTS:(x + 1) * SLOTS, :], he[:, (x * 4 + f) * SLOTS:(x * 4 + f + 1) * SLOTS],
                                       w[:, f * D + c * 512:f * D + (c + 1) * 512], start=f == 0, stop=f == 3)
                        m.then_inc(s["expert_used"], 1)
                    pe.wait_ge(s["gatedT_ready"], t + 1)
                    for i in range(4):
                        pe.wait_ge(s["y_copied"], t * 2 + 2)
                        if i >= 2:
                            pe.wait_ge(s["added"], t * 4 + i - 1)
                        for k in range(2):
                            c = 2 * i + k
                            m = mm(SC[i % 2][:, k * S:(k + 1) * S], ye[:, c * P:(c + 1) * P], gatedT, start=True, stop=True)
                        m.then_inc(s["scattered"], 1)
                pe.reg_add(pairs_done, pairs_done, n)
            pe.wait_ge(s["squares"], 3 * depth + 1)
            column_sum(M[2][:, 0:S], tmp, KD).then_inc(s["norm_sum"], 1)

        @block.scalar
        def _(act):
            def activate(out, src, func, **kw):
                return nc.scalar.activation(out, src, func, **kw)

            def root(src, n, width, out):
                return activate(out, src, ACT.Sqrt, bias=eps, scale=1.0 / n)

            act.wait_ge(s["angle"], 1)
            for i in range(2):
                activate(sin2[:, i * S:(i + 1) * S], rstd[:, 0:S], ACT.Sin)
                m = activate(cos2[:, i * S:(i + 1) * S], rstd[:, S:2 * S], ACT.Sin)
            m.then_inc(s["sin_done"], 1)
            act.wait_ge(s["sin_done"], 1)
            act.wait_ge(s["mem_sum"], 1)
            root(M[2][:, 0:S], D, S, rstd[:, 0:S]).then_inc(s["mem_root"], 1)
            pairs_done = act.alloc_register("pairs_done")
            act.reg_mov(pairs_done, 0)
            with act.Fori(0, depth) as l:
                def norm_root(n):
                    act.wait_ge(s["norm_sum"], l * 3 + n)
                    root(M[2][:, 0:S], D, S, rstd[:, 0:S]).then_inc(s["norm_root"], 1)

                norm_root(1)
                for i in range(2):
                    act.wait_ge(s["proj_done"], l * JOBS + J_CG + i + 1)
                    activate(sg[:, i * 512:(i + 1) * 512], R[J_CG + i][:], ACT.Sigmoid).then_inc(bank_free[J_CG + i], 1)
                for j in range(J_Q, J_V):
                    i = j - J_Q
                    act.wait_ge(s["proj_done"], l * JOBS + j + 1)
                    activate(qk[:, i * 512:(i + 1) * 512], R[j % RB][:], ACT.Copy).then_inc(s["qk_raw"], 1)
                    act.wait_ge(s["qk_raw"], l * 4 + i + 1)
                    act.sem_inc(bank_free[j % RB], 1)
                for i in range(TB):
                    j = J_V + i
                    act.wait_ge(s["proj_done"], l * JOBS + j + 1)
                    activate(v[:, i * 512:(i + 1) * 512], R[j % RB][:], ACT.Copy).then_inc(bank_free[j % RB], 1)
                act.wait_ge(s["z_ready"], l + 1)
                for i in range(2):
                    j = J_SG + i
                    act.wait_ge(s["proj_done"], l * JOBS + j + 1)
                    activate(sg[:, i * 512:(i + 1) * 512], R[j % RB][:], ACT.Sigmoid).then_inc(s["sig_sg"], 1)
                for i in range(8):
                    j = J_G + i
                    act.wait_ge(s["proj_done"], l * JOBS + j + 1)
                    for c in range(2):
                        f = 2 * i + c
                        m = activate(gates[:, f * S:(f + 1) * S], R[j % RB][:, c * S:(c + 1) * S], ACT.Sigmoid,
                                     bias=vcol(act, l, V_BG + f))
                    m.then_inc(bank_free[j % RB], 1)
                    if i == 6:
                        for h in range(2):
                            act.wait_ge(s["r_norm_sum"], l * 2 + h + 1)
                            root(M[2 + h][:], P, 512, rstd[:, h * 512:(h + 1) * 512]).then_inc(s["r_root"], 1)
                for i in range(2):
                    j = J_XK + i
                    act.wait_ge(s["proj_done"], l * JOBS + j + 1)
                    activate(kx[:, i * 512:(i + 1) * 512], R[j % RB][:], ACT.Copy).then_inc(bank_free[j % RB], 1)
                act.wait_ge(s["ln_var"], l + 1)
                act.wait_ge(s["ret_ready"], l + 1)
                root(M[1][:, 0:S], 512, S, rstd[:, 0:S]).then_inc(s["ln_root"], 1)
                for i in range(2):
                    j = J_XV + i
                    act.wait_ge(s["proj_done"], l * JOBS + j + 1)
                    activate(vx[:, i * 512:(i + 1) * 512], R[j % RB][:], ACT.Copy).then_inc(bank_free[j % RB], 1)
                act.wait_ge(s["ln_scaled"], l + 1)
                for c in range(CB):
                    m = activate(tmp[:, c * S:(c + 1) * S], cz[:, c * S:(c + 1) * S], ACT.Sigmoid,
                                 bias=vcol(act, l, V_LB + c))
                m.then_inc(s["ln_sig"], 1)
                norm_root(2)
                for i in range(2):
                    j = J_XQ + i
                    act.wait_ge(s["proj_done"], l * JOBS + j + 1)
                    activate(qx[:, i * 512:(i + 1) * 512], R[j % RB][:], ACT.Copy).then_inc(bank_free[j % RB], 1)
                for h in range(HEADS):
                    act.wait_ge(s["att_max"], l * HEADS + h + 1)
                    for b in range(TB):
                        m = activate(probs[:, (h * TB + b) * S:(h * TB + b + 1) * S], M[h][:, b * S:(b + 1) * S], ACT.Exp,
                                     scale=SCALE, bias=neg_max[:, h * TB + b:h * TB + b + 1],
                                     accum_out=exp_sum[:, h * TB + b:h * TB + b + 1])
                    m.then_inc(s["att_exp"], 1)
                for h in range(HEADS):
                    act.wait_ge(s["att_T"], l * HEADS + h + 1)
                    activate(pT[:, h * 512:(h + 1) * 512], M[h][:], ACT.Copy).then_inc(s["att_pT"], 1)
                norm_root(3)
                act.wait_ge(s["logits"], l + 1)
                activate(score, R[0][:, 0:2 * E], ACT.Sigmoid).then_inc(s["router_sig"], 1)
                for i in range(4):
                    act.wait_ge(s["tok_T"], l * 4 + i + 1)
                    activate(tok[:, i * 512:(i + 1) * 512], M[i][:], ACT.Copy).then_inc(s["tok_ready"], 1)
                n = iterations(act, l)
                pairs = act.snap(pairs_done)
                with act.Fori(0, n) as it:
                    t = act.snap(pairs + it)
                    act.wait_ge(s["gathered"], t * 2 + 1)
                    activate(xg[:, 0:512], GA[0][:], ACT.Copy).then_inc(s["xg_ready"], 1)
                    for x in range(2):
                        act.wait_ge(s["expert_used"], t * RING + RING + 2 * x + 2)
                        activate(sig[:, x * S:(x + 1) * S], GU[x][:, 0:S], ACT.Sigmoid).then_inc(s["up_sig"], 1)
                    act.wait_ge(s["expert_used"], t * RING + 2 * RING)
                    activate(ye[:, 0:512], DN[0][:], ACT.Copy).then_inc(s["y_copied"], 1)
                act.reg_add(pairs_done, pairs_done, n)
            act.wait_ge(s["norm_sum"], 3 * depth + 1)
            root(M[2][:, 0:S], D, S, rstd[:, 0:S]).then_inc(s["norm_root"], 1)

        @block.vector
        def _(dve):
            ve = nc.vector

            def links(name, base, per):
                state = [0]

                def link(ins):
                    state[0] += 1
                    ins.then_inc(s[name], 1)
                    dve.wait_ge(s[name], state[0] if base is None else base * per + state[0])

                return link, state

            def squares(n, name="squares"):
                ve.tensor_tensor(tmp[:], xT[:], xT[:], ALU.mult).then_inc(s[name], 1)

            def normed(out, gain, link):
                link(ve.reciprocal(rstd[:, 0:S], rstd[:, 0:S]))
                for k in range(KD):
                    m = ve.scalar_tensor_tensor(out=out[:, k * S:(k + 1) * S], in0=xT[:, k * S:(k + 1) * S], scalar=gain(k),
                                                in1=rstd[:, 0:S], op0=ALU.mult, op1=ALU.mult)
                return m

            link, _n = links("start_link", None, 0)
            ve.memset(zp[:], 0.0)
            dve.wait_ge(s["const_in"], 48)
            dve.wait_ge(s["pos_in"], 16)
            ang, turns, part = rstd[:, 0:S], rstd[:, S:2 * S], rstd[:, 2 * S:3 * S]
            link(ve.tensor_copy(part, pos_i))
            link(ve.tensor_scalar(ang, part, const[:, C_FREQ:C_FREQ + 1], None, ALU.mult))
            link(ve.tensor_scalar(turns, ang, float(1.0 / TWO_PI), MAGIC, ALU.mult, ALU.add))
            link(ve.tensor_scalar(turns, turns, -MAGIC, None, ALU.add))
            for c in (PI_A, PI_B, PI_C):
                link(ve.scalar_tensor_tensor(out=ang, in0=turns, scalar=-c, in1=ang, op0=ALU.mult, op1=ALU.add))
            link(ve.tensor_scalar(ang, ang, 3.1415925, -3.1415925, ALU.min, ALU.max))
            link(ve.tensor_scalar(turns, ang, -1.0, None, ALU.mult))
            link(ve.tensor_tensor(turns, turns, ang, ALU.max))
            ve.tensor_scalar(turns, turns, -1.0, float(np.pi / 2), ALU.mult, ALU.add).then_inc(s["angle"], 1)
            dve.wait_ge(s["mem_in"], 16)
            ve.tensor_tensor(tmp[:], hT[:], hT[:], ALU.mult).then_inc(s["mem_squares"], 1)
            dve.wait_ge(s["mem_root"], 1)
            link(ve.reciprocal(rstd[:, 0:S], rstd[:, 0:S]))
            for k in range(KD):
                m = ve.tensor_tensor(memhat[:, k * S:(k + 1) * S], hT[:, k * S:(k + 1) * S], rstd[:, 0:S], ALU.mult)
            link(m)
            dve.wait_ge(s["x_in"], 16)
            pairs_done = dve.alloc_register("pairs_done")
            dve.reg_mov(pairs_done, 0)
            with dve.Fori(0, depth) as l:
                link, n_links = links("link", l, DVE_LINKS)

                def next_norm(n, col):
                    squares(n)
                    dve.wait_ge(s["norm_root"], l * 3 + n)
                    normed(hT, lambda k: vcol(dve, l, col + k), link).then_inc(s["normed"], 1)

                def job(j):
                    dve.wait_ge(s["proj_done"], l * JOBS + j + 1)
                    return R[j % RB]

                next_norm(1, V_MIX)
                for i in range(2):
                    src = job(J_CA + i)
                    dve.wait_ge(bank_free[J_CG + i], l * JOBS_OF_BANK[J_CG + i] + 1)
                    for c in range(2):
                        b = 2 * i + c
                        m = ve.tensor_tensor(zp[:, b * ZW + TAPS - 1:(b + 1) * ZW], src[:, c * S:(c + 1) * S],
                                             sg[:, b * S:(b + 1) * S], ALU.mult)
                    m.then_inc(bank_free[(J_CA + i) % RB], 1)
                    dve.wait_ge(bank_free[(J_CA + i) % RB], l * JOBS_OF_BANK[(J_CA + i) % RB] + 1)
                dve.sem_inc(s["z_ready"], 1)
                for w in range(TAPS):
                    for c in range(CB):
                        n = w * CB + c
                        src = zp[:, c * ZW + w:c * ZW + w + S]
                        acc = cz[:, c * S:(c + 1) * S]
                        if w == 0:
                            m = ve.tensor_scalar(acc, src, vcol(dve, l, V_TAP + n), vcol(dve, l, V_CB + c), ALU.mult, ALU.add)
                        else:
                            dve.wait_ge(s["conv_tap"], l * (TAPS * CB) + n - CB + 1)
                            m = ve.scalar_tensor_tensor(out=acc, in0=src, scalar=vcol(dve, l, V_TAP + n), in1=acc,
                                                        op0=ALU.mult, op1=ALU.add)
                        m.then_inc(s["conv_tap"], 1)
                for i in range(4):
                    dve.wait_ge(s["swapped"], l * 4 + i + 1)
                    raw = qk[:, i * 512:(i + 1) * 512]
                    part = tmp[:, i * 512:(i + 1) * 512]
                    ve.tensor_tensor(part, M[i][:], sin2[:], ALU.mult)
                    link(ve.tensor_tensor(raw, raw, cos2[:], ALU.mult))
                    ve.tensor_tensor(raw, raw, part, ALU.add).then_inc(s["rotated"], 1)
                for i in range(2):
                    dve.wait_ge(s["sig_sg"], l * 2 + i + 1)
                    j = J_SG + i
                    half = sg[:, i * 512:(i + 1) * 512]
                    ve.tensor_tensor(half, half, job(j)[:], ALU.mult).then_inc(bank_free[j % RB], 1)
                for h in range(HEADS):
                    dve.wait_ge(s["scores"], l * HEADS + h + 1)
                    decay = const[:, C_DECAY + h * S:C_DECAY + (h + 1) * S]
                    ve.tensor_tensor(sT[:, h * 384:h * 384 + S], M[h][:, 0:S], decay, ALU.mult)
                    ve.tensor_tensor(sT[:, h * 384 + S:h * 384 + 384], M[h][:, S:S + P], decay[:, 0:P], ALU.mult
                                     ).then_inc(s["masked"], 1)
                for i in range(2):
                    dve.wait_ge(s["r_sum"], l * HEADS + 2 * i + 2)
                    link(ve.tensor_copy(r[:, i * 512:(i + 1) * 512], M[i][:]))
                dve.sem_inc(s["r_copied"], 1)
                ve.tensor_tensor(tmp[:, 0:1024], r[:], r[:], ALU.mult).then_inc(s["r_squares"], 1)
                for k in range(KD):
                    m = ve.tensor_scalar(memn[:, k * S:(k + 1) * S], memhat[:, k * S:(k + 1) * S],
                                         vcol(dve, l, V_MEM + k), None, ALU.mult)
                m.then_inc(s["memn_ready"], 1)
                dve.wait_ge(s["r_root"], l * 2 + 2)
                link(ve.reciprocal(rstd[:], rstd[:]))
                for h in range(HEADS):
                    head = r[:, h * S:(h + 1) * S]
                    m = ve.scalar_tensor_tensor(out=head, in0=head, scalar=vcol(dve, l, V_RET + h),
                                                in1=rstd[:, h * S:(h + 1) * S], op0=ALU.mult, op1=ALU.mult)
                link(m)
                dve.wait_ge(bank_free[(J_SG + 1) % RB], l * JOBS_OF_BANK[(J_SG + 1) % RB] + (J_SG + 1) // RB + 1)
                ve.tensor_tensor(r[:], r[:], sg[:], ALU.mult).then_inc(s["ret_ready"], 1)
                dve.wait_ge(s["ln_mean"], l + 1)
                for c in range(CB):
                    blk = cz[:, c * S:(c + 1) * S]
                    m = ve.scalar_tensor_tensor(out=blk, in0=M[0][:, 0:S], scalar=-1.0 / 512, in1=blk, op0=ALU.mult, op1=ALU.add)
                link(m)
                ve.tensor_tensor(tmp[:, 0:1024], cz[:], cz[:], ALU.mult).then_inc(s["ln_squares"], 1)
                dve.wait_ge(s["ln_root"], l + 1)
                link(ve.reciprocal(rstd[:, 0:S], rstd[:, 0:S]))
                for c in range(CB):
                    blk = cz[:, c * S:(c + 1) * S]
                    m = ve.scalar_tensor_tensor(out=blk, in0=blk, scalar=vcol(dve, l, V_LG + c), in1=rstd[:, 0:S],
                                                op0=ALU.mult, op1=ALU.mult)
                m.then_inc(s["ln_scaled"], 1)
                dve.wait_ge(s["ln_sig"], l + 1)
                for c in range(CB):
                    blk = cz[:, c * S:(c + 1) * S]
                    m = ve.scalar_tensor_tensor(out=blk, in0=blk, scalar=vcol(dve, l, V_LB + c), in1=tmp[:, c * S:(c + 1) * S],
                                                op0=ALU.add, op1=ALU.mult)
                m.then_inc(s["conv_ready"], 1)
                for i in range(4):
                    j = J_RET + i
                    half = mixin[:, i * 512:(i + 1) * 512]
                    ve.tensor_tensor(half, job(j)[:], gates[:, i * 512:(i + 1) * 512], ALU.mult).then_inc(bank_free[j % RB], 1)
                for i in range(4):
                    j = J_CONV + i
                    half = mixin[:, i * 512:(i + 1) * 512]
                    part = tmp[:, i * 512:(i + 1) * 512]
                    src = job(j)
                    ve.tensor_tensor(part, src[:], gates[:, 2048 + i * 512:2048 + (i + 1) * 512], ALU.mult
                                     ).then_inc(bank_free[j % RB], 1)
                    dve.wait_ge(bank_free[j % RB], l * JOBS_OF_BANK[j % RB] + j // RB + 1)
                    m = ve.tensor_tensor(half, half, part, ALU.add)
                m.then_inc(s["mix_ready"], 1)

                def add_to_x(j0):
                    for i in range(4):
                        j = j0 + i
                        half = xT[:, i * 512:(i + 1) * 512]
                        ve.tensor_tensor(half, half, job(j)[:], ALU.add).then_inc(bank_free[j % RB], 1)
                        dve.wait_ge(bank_free[j % RB], l * JOBS_OF_BANK[j % RB] + j // RB + 1)

                add_to_x(J_MIX)
                next_norm(2, V_XATTN)
                for h in range(HEADS):
                    dve.wait_ge(s["att_scores"], l * HEADS + h + 1)
                    cols = neg_max[:, h * TB:(h + 1) * TB]
                    link(ve.tensor_reduce(cols, M[h][:].rearrange("p (b m) -> p b m", b=TB), AX, ALU.max))
                    ve.tensor_scalar(cols, cols, -SCALE, None, ALU.mult).then_inc(s["att_max"], 1)
                for h in range(HEADS):
                    dve.wait_ge(s["att_exp"], l * HEADS + h + 1)
                    cols = exp_sum[:, h * TB:(h + 1) * TB]
                    link(ve.reciprocal(cols, cols))
                    for b in range(TB):
                        row = probs[:, (h * TB + b) * S:(h * TB + b + 1) * S]
                        m = ve.tensor_scalar(row, row, exp_sum[:, h * TB + b:h * TB + b + 1], None, ALU.mult)
                    m.then_inc(s["att_probs"], 1)
                for i in range(2):
                    dve.wait_ge(s["att_o"], l * HEADS + 2 * i + 2)
                    ve.tensor_copy(oT[:, i * 512:(i + 1) * 512], M[i][:]).then_inc(s["att_oT"], 1)
                add_to_x(J_XO)
                next_norm(3, V_FFN)

                dve.wait_ge(s["router_sig"], l + 1)
                key4, key16 = const[:, C_KEY4:C_KEY4 + 4], const[:, C_KEY16:C_KEY16 + E]
                for b in range(TB):
                    sc = score[:, b * E:(b + 1) * E]
                    ch = chosen[:, b * E:(b + 1) * E]
                    link(ve.tensor_tensor(sel, sc, glob[:, G_BR:G_BR + E], ALU.add))
                    s4 = sel.rearrange("p (g m) -> p g m", g=4)
                    p4 = sums.rearrange("p (g m) -> p g m", g=4)
                    ve.tensor_tensor(p4[:, :, 0:3], s4[:, :, 0:3], s4[:, :, 1:4], ALU.add)
                    ve.tensor_tensor(p4[:, :, 3:5], s4[:, :, 0:2], s4[:, :, 2:4], ALU.add)
                    link(ve.tensor_tensor(p4[:, :, 5:6], s4[:, :, 0:1], s4[:, :, 3:4], ALU.add))
                    link(ve.tensor_reduce(group, p4, AX, ALU.max))

                    def first_best(values, keys, hot):
                        link(ve.tensor_reduce(best, values, AX, ALU.max))
                        link(ve.scalar_tensor_tensor(out=keyed[:, 0:keys.shape[1]], in0=values, scalar=best, in1=keys,
                                                     op0=ALU.is_equal, op1=ALU.mult))
                        link(ve.tensor_reduce(best, keyed[:, 0:keys.shape[1]], AX, ALU.max))
                        link(ve.tensor_scalar(hot, keys, best, None, ALU.is_equal))

                    first_best(group, key4, ingroup)
                    link(ve.tensor_scalar(ingroup, ingroup, BIG, -BIG, ALU.mult, ALU.add))
                    link(ve.tensor_tensor(s4, s4, ingroup.unsqueeze(2).broadcast_to([P, 4, 4]), ALU.add))
                    first_best(sel, key16, ch)
                    link(ve.scalar_tensor_tensor(out=sel, in0=ch, scalar=-BIG, in1=sel, op0=ALU.mult, op1=ALU.add))
                    first_best(sel, key16, hot2)
                    link(ve.tensor_tensor(ch, ch, hot2, ALU.add))
                    link(ve.tensor_tensor(sel, sc, ch, ALU.mult))
                    link(ve.tensor_reduce(best, sel, AX, ALU.add))
                    link(ve.reciprocal(best, best))
                    link(ve.tensor_scalar(gate[:, b * E:(b + 1) * E], sel, best, None, ALU.mult))
                dve.sem_inc(s["chosen"], 1)
                dve.wait_ge(s["ranks"], l + 1)
                link(ve.scalar_tensor_tensor(out=place, in0=R[1][:, 0:2 * E], scalar=1.0, in1=chosen, op0=ALU.add, op1=ALU.mult))
                link(ve.tensor_scalar(place, place, -1.0, None, ALU.add))
                link(ve.tensor_reduce(best, R[1][:, 2 * E:3 * E], AX, ALU.max))
                steps = const[0:1, C_IOTA + SLOTS:C_IOTA + S].rearrange("p (n m) -> p n m", m=SLOTS)[:, :, 0]
                link(ve.tensor_scalar(keyed[0:1, 0:3], steps, best[0:1, :], None, ALU.is_lt))
                link(ve.tensor_reduce(best[0:1, :], keyed[0:1, 0:3], AX, ALU.add))
                ve.tensor_scalar(count[0:1, 0:1], best[0:1, :], float(PAIRS), float(PAIRS), ALU.mult, ALU.add
                                 ).then_inc(s["sweeps_known"], 1)
                assert n_links[0] == DVE_LINKS, ("DVE_LINKS", n_links[0])

                n = iterations(dve, l)
                pairs = dve.snap(pairs_done)
                with dve.Fori(0, n) as it:
                    t = dve.snap(pairs + it)
                    pair = dve.snap(it % PAIRS)
                    row = dve.snap(it // PAIRS * SLOTS)
                    slots = const[:, bass.ds(row + C_IOTA, SLOTS)]
                    for b in range(TB):
                        for x in range(2):
                            mine = place[:, bass.ds(pair * 2 + (b * E + x), 1)]
                            at = b * P + x * SLOTS
                            ve.tensor_scalar(onehot[:, at:at + SLOTS], slots, mine, None, ALU.is_equal)
                            m = ve.tensor_scalar(gated[:, at:at + SLOTS], slots, mine,
                                                 gate[:, bass.ds(pair * 2 + (b * E + x), 1)], ALU.is_equal, ALU.mult)
                    m.then_inc(s["onehot_ready"], 1)
                    dve.wait_ge(s["gathered"], t * 2 + 2)
                    ve.tensor_copy(xg[:, 512:1024], GA[1][:]).then_inc(s["xg_ready"], 1)
                    dve.wait_ge(s["gatedT_psum"], t + 1)
                    ve.tensor_copy(gatedT, SC[0][:, 0:S]).then_inc(s["gatedT_ready"], 1)
                    for x in range(2):
                        half = he[:, x * S:(x + 1) * S]
                        dve.wait_ge(s["up_sig"], t * 2 + x + 1)
                        ve.tensor_tensor(half, sig[:, x * S:(x + 1) * S], GU[x][:, 0:S], ALU.mult).then_inc(s["pair_link"], 1)
                        dve.wait_ge(s["pair_link"], t * 2 + x + 1)
                        ve.tensor_tensor(half, half, GU[x][:, S:2 * S], ALU.mult).then_inc(s["he_ready"], 1)
                    dve.wait_ge(s["expert_used"], t * RING + 2 * RING)
                    ve.tensor_copy(ye[:, 512:1024], DN[1][:]).then_inc(s["y_copied"], 1)
                    for i in range(4):
                        dve.wait_ge(s["scattered"], t * 4 + i + 1)
                        half = xT[:, i * 512:(i + 1) * 512]
                        ve.tensor_tensor(half, half, SC[i % 2][:], ALU.add).then_inc(s["added"], 1)
                dve.reg_add(pairs_done, pairs_done, n)
                dve.wait_ge(s["added"], dve.snap(pairs_done) * 4)
            link, _n = links("start_link", None, 0)
            squares(0)
            dve.wait_ge(s["norm_root"], 3 * depth + 1)
            ve.reciprocal(rstd[:, 0:S], rstd[:, 0:S]).then_inc(s["mem_squares"], 1)
            dve.wait_ge(s["mem_squares"], 2)
            for k in range(KD):
                m = ve.scalar_tensor_tensor(out=hT[:, k * S:(k + 1) * S], in0=xT[:, k * S:(k + 1) * S],
                                            scalar=glob[:, G_FIN + k:G_FIN + k + 1], in1=rstd[:, 0:S], op0=ALU.mult, op1=ALU.mult)
            m.then_inc(s["finished"], 1)


def constants():
    c = np.zeros((P, C_ALL), np.float32)
    i = np.arange(P)
    c[i, C_ID + i] = 1
    c[:, C_ONE:C_ONE + P] = 1
    half = P // 2
    c[np.arange(half) + half, C_SWAP + np.arange(half)] = -1
    c[np.arange(half), C_SWAP + half + np.arange(half)] = 1
    c[:, C_BEFORE:C_BEFORE + P] = i[:, None] < i[None, :]
    gap = np.arange(S)[None, :] - i[:, None]
    for h in range(HEADS):
        log_gamma = np.log(1.0 - 2.0 ** (-5.0 - h))
        c[:, C_DECAY + h * S:C_DECAY + (h + 1) * S] = np.where(gap >= 0, np.exp(np.maximum(gap, 0) * log_gamma) * SCALE, 0.0)
    c[:, C_IOTA:C_IOTA + S] = np.arange(S)
    c[:, C_KEY4:C_KEY4 + 4] = 4 - np.arange(4)
    c[:, C_KEY16:C_KEY16 + E] = E - np.arange(E)
    c[:, C_FREQ] = np.float32(10000.0) ** (-(i % half).astype(np.float32) / half)
    c[:, C_EPS] = EPS
    return c


def columns(a):
    a = np.asarray(a)
    return np.moveaxis(a.reshape(*a.shape[:-1], -1, P), -1, 0)


def blocks(w, cols):
    rows = w.shape[0]
    return w.reshape(rows // P, P, -1, cols).transpose(2, 1, 0, 3).reshape(-1, P, rows // P * cols)


def kernel(x, mem, positions, norm_mix_g, w_in, b_branch_gate, ret_norm_g, w_ret_out, conv_w, conv_b, conv_ln_g,
           conv_ln_b, w_conv_out, w_mix_out, norm_xattn_g, norm_mem_g, w_xq, w_xkv, w_xo, norm_ffn_g, w_router,
           b_router, w_exp_gate, w_exp_up, w_exp_down, norm_final_g):
    import concourse.bacc as bacc
    from concourse.bass_utils import run_bass_kernel_spmd

    depth = w_in.shape[0]
    vec = np.zeros((P, depth, V_ALL), np.float32)
    for at, a in ((V_MIX, norm_mix_g), (V_XATTN, norm_xattn_g), (V_MEM, norm_mem_g), (V_FFN, norm_ffn_g),
                  (V_BG, b_branch_gate), (V_RET, ret_norm_g), (V_CB, conv_b), (V_LG, conv_ln_g), (V_LB, conv_ln_b)):
        a = columns(a)
        vec[:, :, at:at + a.shape[2]] = a
    vec[:, :, V_TAP:] = columns(conv_w).reshape(P, depth, TAPS * CB)
    glob = np.zeros((P, G_ALL), np.float32)
    glob[:, G_RT:G_RT + KD * E] = np.asarray(w_router).reshape(KD, P, E).transpose(1, 0, 2).reshape(P, -1)
    glob[:, G_BR:G_BR + E] = np.asarray(b_router)[None, :]
    glob[:, G_FIN:G_FIN + KD] = columns(norm_final_g)
    dense = np.empty((depth, DENSE_UNITS, P, UNIT), np.float32)
    experts = np.empty((depth, PAIRS, RING, P, UNIT), np.float32)
    for l in range(depth):
        win = blocks(np.asarray(w_in[l]), 512)
        dense[l, [U_Q, U_K, U_V, U_SG, U_CA, U_CG, U_G0, U_G1, U_G2, U_G3]] = win
        dense[l, U_RET] = blocks(np.asarray(w_ret_out[l]), D)[0]
        dense[l, U_CONV] = blocks(np.asarray(w_conv_out[l]), D)[0]
        dense[l, U_M0:U_M1 + 1] = blocks(np.asarray(w_mix_out[l]), 512)
        dense[l, U_XQ] = blocks(np.asarray(w_xq[l]), 512)[0]
        dense[l, U_XK:U_XV + 1] = blocks(np.asarray(w_xkv[l]), 512)
        dense[l, U_XO] = blocks(np.asarray(w_xo[l]), D)[0]
        for e in range(E):
            x2 = e % 2
            experts[l, e // 2, 2 * x2] = blocks(np.asarray(w_exp_gate[l, e]), 512)[0]
            experts[l, e // 2, 2 * x2 + 1] = blocks(np.asarray(w_exp_up[l, e]), 512)[0]
            experts[l, e // 2, 4 + x2] = blocks(np.asarray(w_exp_down[l, e]), D)[0]
    experts = experts.reshape(depth * PAIRS, RING, P, UNIT)

    def turned(a):
        return np.ascontiguousarray(np.asarray(a)[0].T.reshape(KD, P, S).transpose(1, 0, 2))

    arrays = {
        "x_in": turned(x), "mem_in": turned(mem),
        "positions_in": np.ascontiguousarray(np.broadcast_to(np.asarray(positions)[None, :], (P, S))),
        "constants_in": constants(), "vectors_in": vec.reshape(P, -1), "globals_in": glob,
        "dense_in": dense, "experts_in": experts,
    }
    nc = bacc.Bacc("TRN2", target_bir_lowering=False, num_devices=1)
    args = [nc.dram_tensor(n, a.shape, mybir.dt.from_np(a.dtype), kind="ExternalInput").ap() for n, a in arrays.items()]
    out = nc.dram_tensor("out", (P, KD, S), F32, kind="ExternalOutput").ap()
    build(nc, *args, out)
    got = run_bass_kernel_spmd(nc, [arrays], core_ids=[0]).results[0]["out"]
    return np.ascontiguousarray(got.transpose(2, 1, 0).reshape(1, S, D))
```

```python
from contextlib import ExitStack

import numpy as np
import concourse.bass as bass
from concourse import mybir

P = 128
D = 1024
S = 256
KD = D // P
TB = S // P
HEADS = 4
CB = 4
TAPS = 31
ZW = S + TAPS - 1
E = 16
SLOTS = 64
PAIRS = E // 2
CHUNK = 2048
RAW = 4
SPLIT = 4
DENSE = 36
PAIR = 12
AHEAD = SPLIT
EPS = 1e-6
SCALE = float(P) ** -0.5
BIG = 1e30
TWO_PI = 2.0 * np.pi
PI_A = 6.28125
PI_B = float(np.float32(np.floor((TWO_PI - PI_A) * 2.0 ** 20) / 2.0 ** 20))
PI_C = float(TWO_PI - PI_A - PI_B)
MAGIC = 12582912.0

C_ID, C_ONE, C_SWAP, C_BEFORE = 0, 128, 256, 384
C_DECAY = 512
C_IOTA = C_DECAY + HEADS * S
C_KEY4 = C_IOTA + (S // SLOTS + 1) * P
C_KEY16 = C_KEY4 + 4
C_EPS = C_KEY16 + 16
C_BOTH = C_EPS + 1
C_ALL = C_BOTH + SLOTS

V_MIX, V_XATTN, V_MEM, V_FFN = 0, 8, 16, 24
V_BG = 32
V_RET = 48
V_CB, V_LG, V_LB = 52, 56, 60
V_TAP = 64
V_ALL = V_TAP + TAPS * CB

G_RT, G_BR, G_FREQ = 0, 128, 144
G_ALL = 145

F32 = mybir.dt.float32
F32R = mybir.dt.float32r
I32 = mybir.dt.int32
ALU = mybir.AluOpType
ACT = mybir.ActivationFunctionType
AX = mybir.AxisListType.X

DVE_LINKS = 49

(CH_CG, CH_CA, CH_Q, CH_K, CH_V, CH_SG, CH_G, CH_RET, CH_CONV, CH_MIX, CH_XQ, CH_XO) = (
    0, 2, 4, 6, 8, 10, 12, 21, 23, 26, 31, 34)
CH_XK, CH_XV = (20, 25), (30, 33)
JOBS_OF_CHUNK = [2 if CH_RET <= c < CH_XK[1] or c >= CH_XO else 1 for c in range(DENSE)]
JOB = [sum(JOBS_OF_CHUNK[:c]) for c in range(DENSE + 1)]
JOBS = JOB[DENSE]
RB = 4
JOBS_OF_BANK = [len(range(b, JOBS, RB)) for b in range(RB)]

H_H, H_MEMN, H_R, H_CZ, H_MIX, H_H2, H_O = 0, 2, 4, 5, 6, 8, 10
HALVES = 11
PLAIN = HALVES - 1

TAP_STEPS = [11] * 3 + [8] * 4 + [10] * 6


def build(nc, xT_d, memT_d, pos_d, const_d, vec_d, glob_d, dense_d, experts_d, out_d):
    depth = dense_d.shape[0]
    ctx = ExitStack()
    with ctx:
        def sb(name, cols, dt=F32, rows=P):
            return ctx.enter_context(nc.sbuf_tensor(name, [rows, cols], dt))

        def sem(name):
            return ctx.enter_context(nc.semaphore(name))

        raw = sb("raw", RAW * CHUNK)
        whi = sb("whi", SPLIT * CHUNK, F32R)
        wlo = sb("wlo", SPLIT * CHUNK, F32R)
        a_hi, a_lo = sb("a_hi", KD * S, F32R), sb("a_lo", KD * S, F32R)
        b_hi, b_lo = sb("b_hi", KD * S, F32R), sb("b_lo", KD * S, F32R)
        const = sb("const", C_ALL)
        vec = sb("vec", (depth + 1) * V_ALL)
        glob = sb("glob", G_ALL)
        sin, cos = sb("sin", S), sb("cos", S)
        xT = sb("xT", KD * S)
        gates = sb("gates", 16 * S)
        qk = sb("qk", 2 * HEADS * S)
        v = sb("v", TB * 512)
        sg = sb("sg", HEADS * S)
        zp = sb("zp", CB * ZW)
        cz = sb("cz", CB * S)
        r = sb("r", HEADS * S)
        tmp = sb("tmp", KD * S)
        rstd = sb("rstd", S)
        rmem = sb("rmem", S)
        small = sb("small", 256)
        count = sb("count", 1, I32, 1)
        pos_i = gates[:, 0:S].bitcast(I32)

        sT = tmp[:, 0:HEADS * 384]
        mixin = qk
        qx = sg
        kx = v
        vx = zp
        probs = gates[:, 0:2048]
        pT = gates[:, 2048:4096]
        oT = r
        gated = gates[:, 0:512]
        gatedT = gates[:, 512:1024]
        ye = gates[:, 1024:3072]
        gu = gates[:, 3072:4096]
        silu = cz
        he = r
        xg = b_hi
        onehot = b_lo[:, 0:S]
        he_parts = b_lo[:, S:S + 1024]

        ps = [ctx.enter_context(nc.psum_tensor(f"bank{i}", [P, 512], F32)) for i in range(8)]
        R, M = ps[0:4], ps[4:8]
        GATE, UP, HT, GB = ps[0:4]
        DN = ps[4:8]
        GATHER_BANKS = (GB, GATE, UP, GB)

        ident = const[:, C_ID:C_ID + P]
        ones = const[:, C_ONE:C_ONE + P]
        swap = const[:, C_SWAP:C_SWAP + P]
        before = const[:, C_BEFORE:C_BEFORE + P]
        eps = const[:, C_EPS:C_EPS + 1]
        both = const[:, C_BOTH:C_BOTH + SLOTS]

        names = """const_in pos_in x_in mem_in out_sent hi_done split_done
            mem_squares mem_sum mem_root angle sin_done
            squares norm_sum norm_root normed plain_ready part_hi part_split
            proj_done qk_raw swapped rotated sig_sg scores masked r_sum r_copied r_squares r_norm_sum r_root
            z_made conv_tap ln_mean ln_squares ln_var ln_root ln_scaled ln_sig
            att_scores att_max att_exp att_probs att_T att_pT att_o att_copied
            logits router_sig tok_T tok_hi tok_split chosen ranks sweeps_known count_due
            expert_used zeroed onehot_ready gated_ready gathered xg_ready gate_copied up_copied turned he_silu
            he_split gatedT_psum gatedT_ready y_copied scattered added pair_link
            link start_link""".split()
        s = {n: sem(n) for n in names}
        landed = [sem(f"landed{i}") for i in range(RAW)]
        bank_free = [sem(f"bank_free{i}") for i in range(RB)]

        at = [0]

        def part_of_small(n):
            at[0] += n
            return small[:, at[0] - n:at[0]]

        chosen, score, gate, place = (part_of_small(TB * E) for _ in range(4))
        sel, keyed = part_of_small(TB * E), part_of_small(TB * E)
        sums, group, ingroup, best = part_of_small(48 - 16), part_of_small(8), part_of_small(8), part_of_small(2)
        neg_max, exp_sum = score[:, 0:8], score[:, 8:16]
        hot2 = place

        block = ctx.enter_context(nc.Block())

        def vcol(l, col):
            return vec[:, bass.ds(l * V_ALL + col, 1)]

        def raw_chunk(c):
            return raw[:, (c % RAW) * CHUNK:(c % RAW + 1) * CHUNK]

        def part(w, c):
            return w[:, (c % SPLIT) * CHUNK:(c % SPLIT + 1) * CHUNK]

        def iterations(eng, l):
            eng.wait_ge(s["sweeps_known"], l + 1)
            eng.sem_inc(s["count_due"], 1)
            return eng.value_load(count[0:1, 0:1], min_val=PAIRS, max_val=PAIRS * (S // SLOTS))

        def counter(eng):
            pairs_done = eng.alloc_register("pairs_done")
            eng.reg_mov(pairs_done, 0)
            return pairs_done

        def freed(eng, l, j):
            eng.wait_ge(bank_free[j % RB], l * JOBS_OF_BANK[j % RB] + j // RB + 1)

        @block.sync
        def _(sp):
            def load(c, src, base=None):
                if base is not None:
                    sp.wait_ge(s["split_done"], base + c + 1)
                sp.dma_start(raw_chunk(c), src.rearrange("o p n -> p (o n)")).then_inc(landed[c % RAW], 16)

            sp.dma_start(xT[:].rearrange("p (k t) -> p k t", k=KD), xT_d).then_inc(s["x_in"], 16)
            sp.dma_start(glob[:], glob_d).then_inc(s["pos_in"], 16)
            sp.dma_start(pos_i, pos_d).then_inc(s["pos_in"], 16)
            sp.dma_start(const[:], const_d).then_inc(s["const_in"], 16)
            sp.dma_start(vec[:], vec_d).then_inc(s["const_in"], 16)
            sp.dma_start(qk[:].rearrange("p (k t) -> p k t", k=KD), memT_d).then_inc(s["mem_in"], 16)
            for c in range(AHEAD):
                load(c, dense_d[0:1, c])
            sp.sem_inc(s["split_done"], RAW)
            pairs_done = counter(sp)
            with sp.Fori(0, depth) as l:
                pairs = sp.snap(pairs_done)
                base = sp.snap(l * DENSE + pairs * PAIR)
                for c in range(AHEAD, DENSE):
                    load(c, dense_d[bass.ds(l, 1), c], base)
                for q in range(PAIR):
                    load(DENSE + q, experts_d[bass.ds(l * PAIRS, 1), q], base)
                n = iterations(sp, l)
                with sp.Fori(1, n) as it:
                    loop_base = sp.snap(base + (it * PAIR + DENSE))
                    for q in range(PAIR):
                        load(q, experts_d[bass.ds(l * PAIRS + it % PAIRS, 1), q], loop_base)
                sp.reg_add(pairs_done, pairs_done, n)
                next_base = sp.snap((l + 1) * DENSE + sp.snap(pairs_done) * PAIR)
                for c in range(AHEAD):
                    load(c, dense_d[bass.ds((l + 1) % depth, 1), c], next_base)
                sp.wait_ge(s["normed"], l * 2 + 2)
                sp.dma_start(qk[:].rearrange("p (k t) -> p k t", k=KD), memT_d).then_inc(s["mem_in"], 16)
            sp.wait_ge(s["mem_in"], (depth + 1) * 16)
            sp.wait_ge(s["plain_ready"], depth * PLAIN + 2)
            sp.dma_start(out_d, tmp[:].rearrange("p (k t) -> p k t", k=KD)).then_inc(s["out_sent"], 16)
            sp.wait_ge(s["out_sent"], 16)

        @block.tensor
        def _(pe):
            mm = nc.tensor.matmul

            def column_sum(out, squares, blocks):
                for k in range(blocks):
                    m = mm(out, ones, squares[:, k * S:(k + 1) * S], start=k == 0, stop=k == blocks - 1)
                return m

            def norm_sum(out, n, quarters=range(4)):
                for i in quarters:
                    pe.wait_ge(s["squares"], n * 4 + i + 1)
                    mm(out, ones, tmp[:, 2 * i * S:(2 * i + 1) * S], start=i == 0, stop=False)
                    m = mm(out, ones, tmp[:, (2 * i + 1) * S:(2 * i + 2) * S], start=False, stop=i == 3)
                    if i == 3:
                        m.then_inc(s["norm_sum"], 1)

            pe.wait_ge(s["const_in"], 32)
            norm_sum(HT[:, 0:S], 0)
            pe.wait_ge(s["mem_squares"], 1)
            column_sum(M[2][:, 0:S], gates[:, 2048:4096], KD).then_inc(s["mem_sum"], 1)
            pairs_done = counter(pe)
            with pe.Fori(0, depth) as l:
                pairs = pe.snap(pairs_done)
                base = pe.snap(l * DENSE + pairs * PAIR + RAW)

                def weights(c, chunk_base=base):
                    pe.wait_ge(s["split_done"], chunk_base + c + 1)
                    return part(whi, c), part(wlo, c)

                def bank(j):
                    if j >= RB:
                        freed(pe, l, j - RB)
                    return R[j % RB]

                def half(i):
                    pe.wait_ge(s["part_split"], l * HALVES + i + 1)

                def project(c, src, half0, blocks, rows, first=False):
                    hi, lo = weights(c)
                    for b in range(blocks):
                        j = JOB[c] + b // 2
                        out = (bank(j) if b % 2 == 0 else R[j % RB])[:, (b % 2) * S:(b % 2 + 1) * S]
                        for k in range(rows):
                            if first and b == 0 and k in (0, 4):
                                half(half0 + k // 4)
                            w = slice((k * blocks + b) * P, (k * blocks + b + 1) * P)
                            x = slice(k * S, (k + 1) * S)
                            mm(out, hi[:, w], src[0][:, x], start=k == 0, stop=False)
                            mm(out, hi[:, w], src[1][:, x], start=False, stop=False)
                            m = mm(out, lo[:, w], src[0][:, x], start=False, stop=k == rows - 1)
                        if b % 2 == 1:
                            m.then_inc(s["proj_done"], 1)

                def project_values(c, src):
                    hi, lo = weights(c)
                    out = bank(JOB[c])
                    for b in range(TB):
                        o = out[:, b * S:(b + 1) * S]
                        for k in range(KD):
                            x = slice(k * S + b * P, k * S + b * P + P)
                            w = slice(k * S, (k + 1) * S)
                            mm(o, src[0][:, x], hi[:, w], start=k == 0, stop=False)
                            mm(o, src[1][:, x], hi[:, w], start=False, stop=False)
                            m = mm(o, src[0][:, x], lo[:, w], start=False, stop=k == KD - 1)
                    m.then_inc(s["proj_done"], 1)

                A, B = (a_hi, a_lo), (b_hi, b_lo)
                rc = (a_hi[:, 1024:2048], a_lo[:, 1024:2048])
                for c in range(DENSE):
                    if c in (CH_V, CH_V + 1):
                        project_values(c, A)
                    elif c in CH_XV:
                        project_values(c, B)
                    elif c in CH_XK:
                        project(c, B, H_MEMN, 2, KD, first=c == CH_XK[0])
                    elif c < CH_RET:
                        project(c, A, H_H, 2, KD, first=c == 0)
                    elif c < CH_CONV:
                        if c == CH_RET:
                            half(H_R)
                        project(c, A, 0, 4, CB)
                    elif c < CH_MIX:
                        if c == CH_CONV:
                            half(H_CZ)
                        project(c, rc, 0, 4, CB)
                    elif c < CH_XQ:
                        project(c, A, H_MIX, 2, KD, first=c == CH_MIX)
                    elif c < CH_XO:
                        project(c, A, H_H2, 2, KD, first=c == CH_XQ)
                    else:
                        if c == CH_XO:
                            half(H_O)
                        project(c, A, 0, 4, CB)

                    if CH_K <= c < CH_K + 4:
                        i = c - CH_K
                        pe.wait_ge(s["qk_raw"], l * 4 + i + 1)
                        mm(M[i][:], swap, qk[:, i * 512:(i + 1) * 512], start=True, stop=True).then_inc(s["swapped"], 1)
                    if c == 12:
                        pe.wait_ge(s["rotated"], l * 4 + 4)
                        for h in range(HEADS):
                            q = qk[:, h * S:(h + 1) * S]
                            k = qk[:, (HEADS + h) * S:(HEADS + h + 1) * S]
                            mm(M[h][:, 0:S], k[:, 0:P], q, start=True, stop=True)
                            mm(M[h][:, S:S + P], k[:, P:S], q[:, P:S], start=True, stop=True).then_inc(s["scores"], 1)
                    if c == 15:
                        pe.wait_ge(s["masked"], l * HEADS + HEADS)
                        for h in range(HEADS):
                            out = M[h // 2][:, (h % 2) * S:(h % 2 + 1) * S]
                            mm(out, v[:, h * P:(h + 1) * P], sT[:, h * 384:h * 384 + S], start=True, stop=False)
                            mm(out[:, P:S], v[:, 512 + h * P:512 + (h + 1) * P], sT[:, h * 384 + S:h * 384 + 384],
                               start=False, stop=True).then_inc(s["r_sum"], 1)
                    if c == 17:
                        for i in range(2):
                            pe.wait_ge(s["r_squares"], l * 2 + i + 1)
                            mm(M[2 + i][:], ones, tmp[:, i * 512:(i + 1) * 512], start=True, stop=True
                               ).then_inc(s["r_norm_sum"], 1)
                    if c == 18:
                        pe.wait_ge(s["conv_tap"], (l + 1) * (TAPS * CB))
                        column_sum(M[0][:, 0:S], cz, CB).then_inc(s["ln_mean"], 1)
                    if c == 19:
                        pe.wait_ge(s["ln_squares"], l + 1)
                        column_sum(M[1][:, 0:S], tmp, CB).then_inc(s["ln_var"], 1)
                    if CH_MIX < c <= CH_MIX + 3:
                        norm_sum(M[2][:, 0:S], l * 3 + 1, (c - CH_MIX - 1,) if c < CH_MIX + 3 else (2, 3))
                    if c == CH_XO + 1:
                        norm_sum(M[2][:, 0:S], l * 3 + 2, (0, 1))
                    if c == CH_XQ + 1:
                        freed(pe, l, JOB[CH_XQ])
                        freed(pe, l, JOB[CH_XQ] + 1)
                        for h in range(HEADS):
                            for b in range(TB):
                                m = mm(M[h][:, b * S:(b + 1) * S], qx[:, h * S + b * P:h * S + b * P + P],
                                       kx[:, h * S:(h + 1) * S], start=True, stop=True)
                            m.then_inc(s["att_scores"], 1)
                    if c == CH_XV[1]:
                        for h in range(HEADS):
                            pe.wait_ge(s["att_probs"], l * HEADS + h + 1)
                            for k in range(TB):
                                for b in range(TB):
                                    p = (h * TB + b) * S + k * P
                                    m = nc.tensor.transpose(M[h][:, k * S + b * P:k * S + b * P + P], probs[:, p:p + P], ident)
                            m.then_inc(s["att_T"], 1)
                        freed(pe, l, JOB[CH_XV[1]])
                        for h in range(HEADS):
                            pe.wait_ge(s["att_pT"], l * HEADS + h + 1)
                            for k in range(TB):
                                m = mm(M[h // 2][:, (h % 2) * S:(h % 2 + 1) * S],
                                       vx[:, (h // 2) * 512 + k * S + (h % 2) * P:(h // 2) * 512 + k * S + (h % 2) * P + P],
                                       pT[:, (h * TB + k) * S:(h * TB + k + 1) * S], start=k == 0, stop=k == TB - 1)
                            m.then_inc(s["att_o"], 1)

                norm_sum(M[2][:, 0:S], l * 3 + 2, (2, 3))

                def logits(half_of_features):
                    for b in range(TB):
                        for k in range(half_of_features * 4, half_of_features * 4 + 4):
                            m = mm(R[2 * b][:, 0:E], tmp[:, k * S + b * P:k * S + b * P + P],
                                   glob[:, G_RT + k * E:G_RT + (k + 1) * E], start=k == 0, stop=k == KD - 1)
                    return m

                def turn_tokens(half_of_features):
                    for b in range(TB):
                        for q in range(4):
                            k = half_of_features * 4 + q
                            m = nc.tensor.transpose(M[2 * b + half_of_features][:, q * P:(q + 1) * P],
                                                    tmp[:, k * S + b * P:k * S + b * P + P], ident)
                        m.then_inc(s["tok_T"], 1)

                pe.wait_ge(s["normed"], l * 2 + 1)
                logits(0)
                turn_tokens(0)
                pe.wait_ge(s["normed"], l * 2 + 2)
                logits(1).then_inc(s["logits"], 1)
                turn_tokens(1)
                pe.wait_ge(s["chosen"], l + 1)
                mm(R[1][:, 0:E], before, chosen[:, 0:E], start=True, stop=True)
                mm(R[1][:, E:2 * E], before, chosen[:, E:2 * E], start=True, stop=False)
                mm(R[1][:, E:2 * E], ones, chosen[:, 0:E], start=False, stop=True)
                mm(R[1][:, 2 * E:3 * E], ones, chosen[:, 0:E], start=True, stop=False)
                mm(R[1][:, 2 * E:3 * E], ones, chosen[:, E:2 * E], start=False, stop=True).then_inc(s["ranks"], 1)

                def gather(i, out):
                    src = a_hi if i < 2 else a_lo
                    for k in range(4):
                        f = (i % 2) * 4 + k
                        for b in range(TB):
                            m = mm(out[:, k * P:(k + 1) * P], src[:, b * D + f * P:b * D + (f + 1) * P],
                                   onehot[:, b * P:(b + 1) * P], start=b == 0, stop=b == TB - 1)
                    m.then_inc(s["gathered"], 1)

                def scatter(i):
                    for k in range(2):
                        f = (2 * i + k) * P
                        for x in range(2):
                            m = mm(DN[i][:, k * S:(k + 1) * S], ye[:, x * D + f:x * D + f + P],
                                   gatedT[:, x * S:(x + 1) * S], start=x == 0, stop=x == 1)
                    m.then_inc(s["scattered"], 1)

                pe.wait_ge(s["zeroed"], l + 1)
                pe.wait_ge(s["tok_split"], l * 4 + 4)
                gathers = pe.snap(l + pairs)
                pe.wait_ge(s["onehot_ready"], gathers + 1)
                for i in range(4):
                    if i == 3:
                        pe.wait_ge(s["xg_ready"], gathers * 4 + 1)
                    gather(i, GATHER_BANKS[i])

                n = iterations(pe, l)
                with pe.Fori(0, n) as it:
                    t = pe.snap(it + pairs)
                    g = pe.snap(t + l)
                    pair_base = pe.snap(t * PAIR + (l + 1) * DENSE + RAW)
                    pe.wait_ge(s["xg_ready"], g * 4 + 4)
                    for q in range(PAIR):
                        hi, lo = weights(q, pair_base)
                        if q < 8:
                            x, up, c = q // 4, q % 4 // 2, q % 2
                            if q == 4:
                                pe.wait_ge(s["gate_copied"], t * 2 + 1)
                            if q == 6:
                                pe.wait_ge(s["up_copied"], t * 2 + 1)
                            for k in range(4):
                                tok = xg[:, x * D + (c * 4 + k) * P:x * D + (c * 4 + k + 1) * P]
                                mm((GATE, UP)[up][:], tok, hi[:, k * 512:(k + 1) * 512], start=c == 0 and k == 0, stop=False)
                                m = mm((GATE, UP)[up][:], tok, lo[:, k * 512:(k + 1) * 512], start=False, stop=c == 1 and k == 3)
                        else:
                            x, c = (q - 8) // 2, q % 2
                            if c == 0:
                                pe.wait_ge(s["he_split"], t * 2 + x + 1)
                                if x == 0:
                                    pe.wait_ge(s["added"], g * 4 + 4)
                            for k in range(2):
                                rows = he_parts[:, x * 512 + (c * 2 + k) * P:x * 512 + (c * 2 + k + 1) * P]
                                for o in range(2):
                                    w = slice(k * D + o * 512, k * D + (o + 1) * 512)
                                    mm(DN[2 * x + o][:], rows, hi[:, w], start=c == 0 and k == 0, stop=False)
                                    m = mm(DN[2 * x + o][:], rows, lo[:, w], start=False, stop=c == 1 and k == 1)
                        m.then_inc(s["expert_used"], 1)
                        if 1 <= q <= 4:
                            if q == 1:
                                pe.wait_ge(s["y_copied"], t * 4 + 4 * (l + 1))
                            scatter(q - 1)
                        if q == 6:
                            pe.wait_ge(s["gated_ready"], t + 1)
                            for x in range(2):
                                for b in range(TB):
                                    m = nc.tensor.transpose(GB[:, x * S + b * P:x * S + b * P + P],
                                                            gated[:, (b * 2 + x) * P:(b * 2 + x + 1) * P], ident)
                            m.then_inc(s["gatedT_psum"], 1)
                        if q == 7:
                            pe.wait_ge(s["gatedT_ready"], t + 1)
                            pe.wait_ge(s["onehot_ready"], g + 2)
                            gather(0, GB)
                        if q in (5, 7):
                            x = q // 7
                            pe.wait_ge(s["gate_copied"], t * 2 + x + 1)
                            pe.wait_ge(s["up_copied"], t * 2 + x + 1)
                            if x == 1:
                                pe.wait_ge(s["he_split"], t * 2 + 1)
                            for f in range(8):
                                m = mm(HT[:, f * SLOTS:(f + 1) * SLOTS], gu[:, f * P:(f + 1) * P], both, start=True, stop=True)
                            m.then_inc(s["turned"], 1)
                        if 8 <= q <= 10:
                            if q == 10:
                                pe.wait_ge(s["xg_ready"], g * 4 + 5)
                            gather(q - 7, GATHER_BANKS[q - 7])
                pe.reg_add(pairs_done, pairs_done, n)
                after = pe.snap(pairs_done)
                pe.wait_ge(s["y_copied"], after * 4 + 4 * (l + 1))
                for i in range(4):
                    scatter(i)
                norm_sum(HT[:, 0:S], l * 3 + 3)

        @block.scalar
        def _(act):
            activate = nc.scalar.activation

            def copy(out, src):
                return activate(out, src, ACT.Copy)

            def square(i):
                q = slice(i * 512, (i + 1) * 512)
                activate(tmp[:, q], xT[:, q], ACT.Square, scale=D ** -0.5).then_inc(s["squares"], 1)

            def root(out, mean):
                return activate(out, mean, ACT.Sqrt, bias=eps)

            def norm_root(l, n, bank):
                act.wait_ge(s["norm_sum"], l * 3 + n + 1)
                root(rstd[:], bank[:, 0:S]).then_inc(s["norm_root"], 1)

            def round_half(l, i, dst, src):
                act.wait_ge(s["plain_ready"], l * PLAIN + i + 1)
                copy(dst, src).then_inc(s["part_hi"], 1)

            def round_h(l):
                for i in range(2):
                    h = slice(i * 1024, (i + 1) * 1024)
                    round_half(l, H_H + i, a_hi[:, h], tmp[:, h])

            act.wait_ge(s["x_in"], 16)
            for i in range(4):
                square(i)
            act.wait_ge(s["const_in"], 32)
            norm_root(0, 0, HT)
            act.wait_ge(s["angle"], 1)
            activate(sin[:], gates[:, 256:512], ACT.Sin)
            activate(cos[:], gates[:, 512:768], ACT.Sin).then_inc(s["sin_done"], 1)
            act.wait_ge(s["mem_in"], 16)
            activate(gates[:, 2048:4096], qk[:], ACT.Square, scale=D ** -0.5).then_inc(s["mem_squares"], 1)
            act.wait_ge(landed[0], 16)
            copy(part(whi, 0), raw_chunk(0)).then_inc(s["hi_done"], 1)
            round_h(0)
            for c in range(1, AHEAD):
                act.wait_ge(landed[c], 16)
                copy(part(whi, c), raw_chunk(c)).then_inc(s["hi_done"], 1)
            act.wait_ge(s["mem_sum"], 1)
            root(rmem[:], M[2][:, 0:S]).then_inc(s["mem_root"], 1)
            pairs_done = counter(act)
            with act.Fori(0, depth) as l:
                pairs = act.snap(pairs_done)
                rounds = act.snap(l * (DENSE // RAW) + pairs * (PAIR // RAW))

                def round_chunk(c, from_round):
                    act.wait_ge(landed[c % RAW], (from_round + c // RAW + 1) * 16)
                    copy(part(whi, c), raw_chunk(c)).then_inc(s["hi_done"], 1)

                for c in range(AHEAD, DENSE + AHEAD):
                    u = c - AHEAD
                    act.wait_ge(s["proj_done"], l * JOBS + JOB[u + 1])
                    src = R[JOB[u] % RB]
                    free = bank_free[JOB[u] % RB]
                    if u < CH_CA:
                        activate(sg[:, u * 512:(u + 1) * 512], src[:], ACT.Sigmoid).then_inc(free, 1)
                    if u in (1, 2):
                        i = u - 1
                        round_half(l, H_MEMN + i, b_hi[:, i * 1024:(i + 1) * 1024], qk[:, i * 1024:(i + 1) * 1024])
                    if CH_Q <= u < CH_V:
                        i = u - CH_Q
                        if i == 0:
                            act.wait_ge(s["part_split"], l * HALVES + H_MEMN + 2)
                        copy(qk[:, i * 512:(i + 1) * 512], src[:]).then_inc(s["qk_raw"], 1)
                        act.wait_ge(s["qk_raw"], l * 4 + i + 1)
                        act.sem_inc(free, 1)
                    if CH_V <= u < CH_SG:
                        i = u - CH_V
                        copy(v[:].rearrange("p (b n) -> p b n", b=TB)[:, :, i * S:(i + 1) * S],
                             src[:].rearrange("p (b n) -> p b n", b=TB)).then_inc(free, 1)
                    if CH_SG <= u < CH_G:
                        i = u - CH_SG
                        if i == 0:
                            act.wait_ge(s["z_made"], l * 2 + 2)
                        activate(sg[:, i * 512:(i + 1) * 512], src[:], ACT.Sigmoid).then_inc(s["sig_sg"], 1)
                    if CH_G <= u < CH_XK[0]:
                        i = u - CH_G
                        for k in range(2):
                            f = 2 * i + k
                            m = activate(gates[:, f * S:(f + 1) * S], src[:, k * S:(k + 1) * S], ACT.Sigmoid,
                                         bias=vcol(l, V_BG + f))
                        m.then_inc(free, 1)
                    if u in CH_XK:
                        i = CH_XK.index(u)
                        copy(kx[:, i * 512:(i + 1) * 512], src[:]).then_inc(free, 1)
                    if u in CH_XV:
                        i = CH_XV.index(u)
                        copy(vx[:, i * 512:(i + 1) * 512], src[:]).then_inc(free, 1)
                    if CH_XQ <= u < CH_XO and u not in CH_XV:
                        i = u - CH_XQ
                        copy(qx[:, i * 512:(i + 1) * 512], src[:]).then_inc(free, 1)
                    round_chunk(c, rounds)
                    if u == 15:
                        for i in range(2):
                            act.wait_ge(s["r_sum"], l * HEADS + 2 * i + 2)
                            copy(r[:, i * 512:(i + 1) * 512], M[i][:]).then_inc(s["r_copied"], 1)
                    if u == 17:
                        for i in range(2):
                            act.wait_ge(s["r_norm_sum"], l * 2 + i + 1)
                            root(tmp[:, 1024 + i * 512:1024 + (i + 1) * 512], M[2 + i][:]).then_inc(s["r_root"], 1)
                    if u == 19:
                        act.wait_ge(s["ln_var"], l + 1)
                        root(rstd[:], M[1][:, 0:S]).then_inc(s["ln_root"], 1)
                        round_half(l, H_R, a_hi[:, 0:1024], r[:])
                    if u == 20:
                        act.wait_ge(s["ln_scaled"], l + 1)
                        for k in range(CB):
                            m = activate(tmp[:, 1024 + k * S:1024 + (k + 1) * S], cz[:, k * S:(k + 1) * S], ACT.Sigmoid,
                                         bias=vcol(l, V_LB + k))
                        m.then_inc(s["ln_sig"], 1)
                    if u == 21:
                        round_half(l, H_CZ, a_hi[:, 1024:2048], cz[:])
                    if CH_CONV <= u < CH_XK[1]:
                        i = u - CH_CONV
                        round_half(l, H_MIX + i, a_hi[:, i * 1024:(i + 1) * 1024], mixin[:, i * 1024:(i + 1) * 1024])
                    if CH_MIX <= u < CH_MIX + 4:
                        freed(act, l, JOB[u])
                        square(u - CH_MIX)
                    if u == CH_MIX + 3:
                        norm_root(l, 1, M[2])
                        for i in range(2):
                            round_half(l, H_H2 + i, a_hi[:, i * 1024:(i + 1) * 1024], tmp[:, i * 1024:(i + 1) * 1024])
                    if u == CH_XQ + 1:
                        for h in range(HEADS):
                            act.wait_ge(s["att_max"], l * HEADS + h + 1)
                            for b in range(TB):
                                i = h * TB + b
                                m = activate(probs[:, i * S:(i + 1) * S], M[h][:, b * S:(b + 1) * S], ACT.Exp, scale=SCALE,
                                             bias=neg_max[:, i:i + 1], accum_out=exp_sum[:, i:i + 1])
                            m.then_inc(s["att_exp"], 1)
                    if u == CH_XV[1]:
                        for h in range(HEADS):
                            act.wait_ge(s["att_T"], l * HEADS + h + 1)
                            copy(pT[:, h * 512:(h + 1) * 512], M[h][:]).then_inc(s["att_pT"], 1)
                        for i in range(2):
                            h = slice(i * 512, (i + 1) * 512)
                            act.wait_ge(s["att_o"], l * HEADS + 2 * i + 2)
                            m = copy(a_hi[:, h], M[i][:])
                        m.then_inc(s["part_hi"], 1)
                    if u >= CH_XO:
                        for j in (JOB[u], JOB[u] + 1):
                            freed(act, l, j)
                            square(j - JOB[CH_XO])

                norm_root(l, 2, M[2])
                act.wait_ge(s["logits"], l + 1)
                for b in range(TB):
                    m = activate(score[:, b * E:(b + 1) * E], R[2 * b][:, 0:E], ACT.Sigmoid)
                m.then_inc(s["router_sig"], 1)
                for n, i in enumerate((0, 2, 1, 3)):
                    act.wait_ge(s["tok_T"], l * 4 + n + 1)
                    copy(a_hi[:, i * 512:(i + 1) * 512], M[i][:]).then_inc(s["tok_hi"], 1)
                g0 = act.snap(l + pairs)
                act.sem_inc(s["y_copied"], 4)

                def keep_gathered(i, g, src):
                    act.wait_ge(s["gathered"], g * 4 + i + 1)
                    dst = xg[:].rearrange("p (x k h n) -> p x k h n", x=2, k=KD, h=2)
                    for x in range(2):
                        m = copy(dst[:, x, (i % 2) * 4:(i % 2) * 4 + 4, i // 2, :],
                                 src[:].rearrange("p (k x n) -> p k x n", k=4, x=2)[:, :, x, :])
                    m.then_inc(s["xg_ready"], 1)

                for i in range(4):
                    keep_gathered(i, g0, GATHER_BANKS[i])
                n = iterations(act, l)
                with act.Fori(0, n) as it:
                    t = act.snap(pairs + it)
                    g = act.snap(t + l)
                    pair_rounds = act.snap((l + 1) * (DENSE // RAW) + t * (PAIR // RAW))
                    for q in range(PAIR):
                        act.wait_ge(s["expert_used"], t * PAIR + q + 1)
                        if q == 1:
                            copy(gu[:, 0:512], GATE[:]).then_inc(s["gate_copied"], 1)
                        if q in (3, 7):
                            copy(gu[:, 512:1024], UP[:]).then_inc(s["up_copied"], 1)
                        if q in (9, 11):
                            x = (q - 9) // 2
                            for o in range(2):
                                copy(ye[:, x * D + o * 512:x * D + (o + 1) * 512], DN[2 * x + o][:]).then_inc(s["y_copied"], 1)
                        round_chunk(q + AHEAD, pair_rounds)
                        if q in (5, 7):
                            x = q // 7
                            act.wait_ge(s["turned"], t * 2 + x + 1)
                            activate(silu[:, x * S:(x + 1) * S], HT[:, 0:S], ACT.Silu).then_inc(s["he_silu"], 1)
                        if q == 5:
                            copy(gu[:, 0:512], GATE[:]).then_inc(s["gate_copied"], 1)
                        if q == 6:
                            act.wait_ge(s["gatedT_psum"], t + 1)
                            copy(gatedT, GB[:]).then_inc(s["gatedT_ready"], 1)
                        if 7 <= q <= 10:
                            keep_gathered(q - 7, g + 1, GATHER_BANKS[q - 7])
                act.reg_add(pairs_done, pairs_done, n)
                steps_done = act.snap((act.snap(pairs_done) + l) * 4)
                for i in range(4):
                    act.wait_ge(s["added"], steps_done + i + 1)
                    square(i)
                norm_root(act.snap(l + 1), 0, HT)
                round_h(act.snap(l + 1))

        @block.vector
        def _(dve):
            ve = nc.vector

            def links(name, base, per):
                state = [0]

                def link(ins):
                    state[0] += 1
                    ins.then_inc(s[name], 1)
                    dve.wait_ge(s[name], state[0] if base is None else base * per + state[0])

                return link, state

            def rest(out, src, hi):
                return ve.tensor_tensor(out, src, hi.bitcast(F32), ALU.subtract)

            def norm(l, n, col, link, name):
                dve.wait_ge(s["norm_root"], l * 3 + n + 1)
                link(ve.reciprocal(rstd[:], rstd[:]))
                for k in range(KD):
                    m = ve.scalar_tensor_tensor(out=tmp[:, k * S:(k + 1) * S], in0=xT[:, k * S:(k + 1) * S],
                                                scalar=vcol(l, col + k), in1=rstd[:], op0=ALU.mult, op1=ALU.mult)
                    if k % 4 == 3:
                        m.then_inc(s[name], 1)

            def rest_of_half(l, i, dst, src, hi):
                dve.wait_ge(s["part_hi"], l * HALVES + i + 1)
                rest(dst, src, hi).then_inc(s["part_split"], 1)

            def rest_of_h(l):
                for i in range(2):
                    h = slice(i * 1024, (i + 1) * 1024)
                    rest_of_half(l, H_H + i, a_lo[:, h], tmp[:, h], a_hi[:, h])

            link, _ = links("start_link", None, 0)
            dve.wait_ge(s["pos_in"], 32)
            ang, turns, pos = gates[:, 256:512], gates[:, 512:768], gates[:, 768:1024]
            link(ve.tensor_copy(pos, pos_i))
            link(ve.tensor_scalar(ang, pos, glob[:, G_FREQ:G_FREQ + 1], None, ALU.mult))
            link(ve.tensor_scalar(turns, ang, float(1.0 / TWO_PI), MAGIC, ALU.mult, ALU.add))
            link(ve.tensor_scalar(turns, turns, -MAGIC, None, ALU.add))
            for c in (PI_A, PI_B, PI_C):
                link(ve.scalar_tensor_tensor(out=ang, in0=turns, scalar=-c, in1=ang, op0=ALU.mult, op1=ALU.add))
            link(ve.tensor_scalar(ang, ang, 3.1415925, -3.1415925, ALU.min, ALU.max))
            link(ve.tensor_scalar(turns, ang, -1.0, None, ALU.mult))
            link(ve.tensor_tensor(turns, turns, ang, ALU.max))
            ve.tensor_scalar(turns, turns, -1.0, float(np.pi / 2), ALU.mult, ALU.add).then_inc(s["angle"], 1)
            dve.wait_ge(s["x_in"], 16)
            dve.wait_ge(s["const_in"], 32)
            norm(0, 0, V_MIX, link, "plain_ready")
            for c in range(AHEAD):
                dve.wait_ge(s["hi_done"], c + 1)
                rest(part(wlo, c), raw_chunk(c), part(whi, c)).then_inc(s["split_done"], 1)
                if c == 0:
                    rest_of_h(0)
            dve.wait_ge(s["mem_root"], 1)
            link(ve.reciprocal(rmem[:], rmem[:]))
            pairs_done = counter(dve)
            with dve.Fori(0, depth) as l:
                link, n_links = links("link", l, DVE_LINKS)
                taps_done = 0
                pairs = dve.snap(pairs_done)
                base = dve.snap(l * DENSE + pairs * PAIR)

                def job(j):
                    return R[j % RB]

                def rest_of_chunk(c, chunk_base):
                    dve.wait_ge(s["hi_done"], chunk_base + c + 1)
                    rest(part(wlo, c), raw_chunk(c), part(whi, c)).then_inc(s["split_done"], 1)

                def add_to_x(j):
                    i = j - (JOB[CH_MIX] if j < JOB[CH_XQ] else JOB[CH_XO])
                    q = slice(i * 512, (i + 1) * 512)
                    ve.tensor_tensor(xT[:, q], xT[:, q], job(j)[:], ALU.add).then_inc(bank_free[j % RB], 1)

                for c in range(AHEAD, DENSE + AHEAD):
                    u = c - AHEAD
                    dve.wait_ge(s["proj_done"], l * JOBS + JOB[u + 1])
                    if u == 0:
                        ve.memset(zp[:].rearrange("p (c z) -> p c z", c=CB)[:, :, 0:TAPS - 1], 0.0)
                        dve.wait_ge(s["mem_in"], (l + 1) * 16)
                        for k in range(KD):
                            m = ve.scalar_tensor_tensor(out=qk[:, k * S:(k + 1) * S], in0=qk[:, k * S:(k + 1) * S],
                                                        scalar=vcol(l, V_MEM + k), in1=rmem[:], op0=ALU.mult, op1=ALU.mult)
                            if k % 4 == 3:
                                m.then_inc(s["plain_ready"], 1)
                    if u in (2, 3):
                        h = slice((u - 2) * 1024, (u - 1) * 1024)
                        rest_of_half(l, H_MEMN + u - 2, b_lo[:, h], qk[:, h], b_hi[:, h])
                    if CH_CA <= u < CH_Q:
                        i = u - CH_CA
                        freed(dve, l, JOB[CH_CG] + i)
                        for k in range(2):
                            b = 2 * i + k
                            m = ve.tensor_tensor(zp[:, b * ZW + TAPS - 1:(b + 1) * ZW], job(JOB[u])[:, k * S:(k + 1) * S],
                                                 sg[:, b * S:(b + 1) * S], ALU.mult)
                        m.then_inc(s["z_made"], 1)
                        dve.wait_ge(s["z_made"], l * 2 + i + 1)
                        dve.sem_inc(bank_free[JOB[u] % RB], 1)
                    if 7 <= u <= 10:
                        i = u - 7
                        dve.wait_ge(s["swapped"], l * 4 + i + 1)
                        x = qk[:, i * 512:(i + 1) * 512].rearrange("p (h t) -> p h t", h=2)
                        y = tmp[:, i * 512:(i + 1) * 512].rearrange("p (h t) -> p h t", h=2)
                        two = [P, 2, S]
                        ve.tensor_tensor(y, M[i][:].rearrange("p (h t) -> p h t", h=2), sin[:].unsqueeze(1).broadcast_to(two),
                                         ALU.mult)
                        link(ve.tensor_tensor(x, x, cos[:].unsqueeze(1).broadcast_to(two), ALU.mult))
                        ve.tensor_tensor(x, x, y, ALU.add).then_inc(s["rotated"], 1)
                    if u in (11, 12):
                        i = u - 11
                        dve.wait_ge(s["sig_sg"], l * 2 + i + 1)
                        j = JOB[CH_SG] + i
                        h = sg[:, i * 512:(i + 1) * 512]
                        ve.tensor_tensor(h, h, job(j)[:], ALU.mult).then_inc(bank_free[j % RB], 1)
                    if u == 13:
                        for h in range(HEADS):
                            dve.wait_ge(s["scores"], l * HEADS + h + 1)
                            decay = const[:, C_DECAY + h * S:C_DECAY + (h + 1) * S]
                            ve.tensor_tensor(sT[:, h * 384:h * 384 + S], M[h][:, 0:S], decay, ALU.mult)
                            ve.tensor_tensor(sT[:, h * 384 + S:h * 384 + 384], M[h][:, S:S + P], decay[:, 0:P], ALU.mult
                                             ).then_inc(s["masked"], 1)
                    if u == 16:
                        for i in range(2):
                            dve.wait_ge(s["r_copied"], l * 2 + i + 1)
                            h = slice(i * 512, (i + 1) * 512)
                            ve.scalar_tensor_tensor(out=tmp[:, h], in0=r[:, h], scalar=1.0 / P, in1=r[:, h],
                                                    op0=ALU.mult, op1=ALU.mult).then_inc(s["r_squares"], 1)
                    if u == 18:
                        rr = tmp[:, 1024:2048]
                        for i in range(2):
                            dve.wait_ge(s["r_root"], l * 2 + i + 1)
                            m = ve.reciprocal(rr[:, i * 512:(i + 1) * 512], rr[:, i * 512:(i + 1) * 512])
                        link(m)
                        for h in range(HEADS):
                            head = r[:, h * S:(h + 1) * S]
                            m = ve.scalar_tensor_tensor(out=head, in0=head, scalar=vcol(l, V_RET + h),
                                                        in1=rr[:, h * S:(h + 1) * S], op0=ALU.mult, op1=ALU.mult)
                        link(m)
                        ve.tensor_tensor(r[:], r[:], sg[:], ALU.mult).then_inc(s["plain_ready"], 1)
                        dve.wait_ge(s["ln_mean"], l + 1)
                        for k in range(CB):
                            blk = cz[:, k * S:(k + 1) * S]
                            m = ve.scalar_tensor_tensor(out=blk, in0=M[0][:, 0:S], scalar=-1.0 / 512, in1=blk,
                                                        op0=ALU.mult, op1=ALU.add)
                        link(m)
                        ve.scalar_tensor_tensor(out=tmp[:, 0:1024], in0=cz[:], scalar=1.0 / 512, in1=cz[:],
                                                op0=ALU.mult, op1=ALU.mult).then_inc(s["ln_squares"], 1)
                    if u == 20:
                        rest_of_half(l, H_R, a_lo[:, 0:1024], r[:], a_hi[:, 0:1024])
                        dve.wait_ge(s["ln_root"], l + 1)
                        link(ve.reciprocal(rstd[:], rstd[:]))
                        for k in range(CB):
                            blk = cz[:, k * S:(k + 1) * S]
                            m = ve.scalar_tensor_tensor(out=blk, in0=blk, scalar=vcol(l, V_LG + k), in1=rstd[:],
                                                        op0=ALU.mult, op1=ALU.mult)
                        m.then_inc(s["ln_scaled"], 1)
                    if u == 21:
                        dve.wait_ge(s["ln_sig"], l + 1)
                        for k in range(CB):
                            blk = cz[:, k * S:(k + 1) * S]
                            m = ve.scalar_tensor_tensor(out=blk, in0=blk, scalar=vcol(l, V_LB + k),
                                                        in1=tmp[:, 1024 + k * S:1024 + (k + 1) * S], op0=ALU.add, op1=ALU.mult)
                        m.then_inc(s["plain_ready"], 1)
                    if u == 22:
                        rest_of_half(l, H_CZ, a_lo[:, 1024:2048], cz[:], a_hi[:, 1024:2048])
                    if CH_RET <= u < CH_CONV:
                        for i in range(2):
                            j = JOB[u] + i
                            q = slice((j - JOB[CH_RET]) * 512, (j - JOB[CH_RET] + 1) * 512)
                            ve.tensor_tensor(mixin[:, q], job(j)[:], gates[:, q], ALU.mult).then_inc(bank_free[j % RB], 1)
                    if CH_CONV <= u < CH_XK[1]:
                        for i in range(2):
                            j = JOB[u] + i
                            n = j - JOB[CH_CONV]
                            q = slice(n * 512, (n + 1) * 512)
                            ve.tensor_tensor(tmp[:, q], job(j)[:], gates[:, 2048 + n * 512:2048 + (n + 1) * 512], ALU.mult
                                             ).then_inc(bank_free[j % RB], 1)
                            freed(dve, l, j)
                            m = ve.tensor_tensor(mixin[:, q], mixin[:, q], tmp[:, q], ALU.add)
                        m.then_inc(s["plain_ready"], 1)
                    if CH_MIX <= u < CH_MIX + 4:
                        add_to_x(JOB[u])
                    if u >= CH_XO:
                        add_to_x(JOB[u])
                        add_to_x(JOB[u] + 1)
                    rest_of_chunk(c, base)
                    if CH_Q <= u < CH_Q + len(TAP_STEPS):
                        for n in range(taps_done, min(taps_done + TAP_STEPS[u - CH_Q], TAPS * CB)):
                            w, k = divmod(n, CB)
                            src = zp[:, k * ZW + w:k * ZW + w + S]
                            acc = cz[:, k * S:(k + 1) * S]
                            if w == 0:
                                m = ve.tensor_scalar(acc, src, vcol(l, V_TAP + n), vcol(l, V_CB + k), ALU.mult, ALU.add)
                            else:
                                dve.wait_ge(s["conv_tap"], l * (TAPS * CB) + n - CB + 1)
                                m = ve.scalar_tensor_tensor(out=acc, in0=src, scalar=vcol(l, V_TAP + n), in1=acc,
                                                            op0=ALU.mult, op1=ALU.add)
                            m.then_inc(s["conv_tap"], 1)
                        taps_done += TAP_STEPS[u - CH_Q]
                    if CH_CONV <= u < CH_XK[1]:
                        i = u - CH_CONV
                        h = slice(i * 1024, (i + 1) * 1024)
                        rest_of_half(l, H_MIX + i, a_lo[:, h], mixin[:, h], a_hi[:, h])
                    if u == CH_MIX + 3:
                        norm(l, 1, V_XATTN, link, "plain_ready")
                        for i in range(2):
                            h = slice(i * 1024, (i + 1) * 1024)
                            rest_of_half(l, H_H2 + i, a_lo[:, h], tmp[:, h], a_hi[:, h])
                    if u == CH_XQ + 1:
                        for h in range(HEADS):
                            dve.wait_ge(s["att_scores"], l * HEADS + h + 1)
                            cols = neg_max[:, h * TB:(h + 1) * TB]
                            link(ve.tensor_reduce(cols, M[h][:].rearrange("p (b m) -> p b m", b=TB), AX, ALU.max))
                            ve.tensor_scalar(cols, cols, -SCALE, None, ALU.mult).then_inc(s["att_max"], 1)
                        for h in range(HEADS):
                            dve.wait_ge(s["att_exp"], l * HEADS + h + 1)
                            cols = exp_sum[:, h * TB:(h + 1) * TB]
                            link(ve.reciprocal(cols, cols))
                            for b in range(TB):
                                i = h * TB + b
                                row = probs[:, i * S:(i + 1) * S]
                                m = ve.tensor_scalar(row, row, exp_sum[:, i:i + 1], None, ALU.mult)
                            m.then_inc(s["att_probs"], 1)
                    if u == CH_XV[1]:
                        dve.wait_ge(s["part_hi"], l * HALVES + H_O + 1)
                        for i in range(2):
                            h = slice(i * 512, (i + 1) * 512)
                            m = rest(a_lo[:, h], M[i][:], a_hi[:, h])
                        m.then_inc(s["part_split"], 1)

                norm(l, 2, V_FFN, link, "normed")
                ve.memset(ye, 0.0)
                ve.memset(gatedT, 0.0).then_inc(s["zeroed"], 1)

                def rest_of_tokens(n, i):
                    dve.wait_ge(s["tok_hi"], l * 4 + n + 1)
                    q = slice(i * 512, (i + 1) * 512)
                    rest(a_lo[:, q], M[i][:], a_hi[:, q]).then_inc(s["tok_split"], 1)

                rest_of_tokens(0, 0)
                rest_of_tokens(1, 2)
                dve.wait_ge(s["router_sig"], l + 1)
                by16, by4 = [P, TB, E], [P, TB, 4]
                score3, sel3, keyed3, ch3, hot3, gate3 = (a.rearrange("p (b e) -> p b e", b=TB)
                                                          for a in (score, sel, keyed, chosen, hot2, gate))
                group3, in3 = (a.rearrange("p (b g) -> p b g", b=TB) for a in (group, ingroup))
                key4 = const[:, C_KEY4:C_KEY4 + 4].unsqueeze(1).broadcast_to(by4)
                key16 = const[:, C_KEY16:C_KEY16 + E].unsqueeze(1).broadcast_to(by16)
                link(ve.tensor_tensor(sel3, score3, glob[:, G_BR:G_BR + E].unsqueeze(1).broadcast_to(by16), ALU.add))
                s4 = sel.rearrange("p (g m) -> p g m", m=4)
                p4 = keyed.rearrange("p (g m) -> p g m", m=4)
                ve.tensor_tensor(p4[:, :, 0:3], s4[:, :, 0:3], s4[:, :, 1:4], ALU.add)
                ve.tensor_tensor(sums.rearrange("p (g m) -> p g m", m=4)[:, :, 0:2], s4[:, :, 0:2], s4[:, :, 2:4], ALU.add)
                link(ve.tensor_tensor(p4[:, :, 3:4], s4[:, :, 0:1], s4[:, :, 3:4], ALU.add))
                link(ve.tensor_tensor(p4[:, :, 0:2], p4[:, :, 0:2], sums.rearrange("p (g m) -> p g m", m=4)[:, :, 0:2], ALU.max))
                link(ve.tensor_reduce(group, p4, AX, ALU.max))

                def first_best(values, keys, shape, hot, scratch):
                    spread = best.unsqueeze(2).broadcast_to(shape)
                    link(ve.tensor_reduce(best, values, AX, ALU.max))
                    link(ve.tensor_tensor(scratch, values, spread, ALU.is_equal))
                    link(ve.tensor_tensor(scratch, scratch, keys, ALU.mult))
                    link(ve.tensor_reduce(best, scratch, AX, ALU.max))
                    link(ve.tensor_tensor(hot, keys, spread, ALU.is_equal))

                first_best(group3, key4, by4, in3, sums[:, 0:8].rearrange("p (b g) -> p b g", b=TB))
                link(ve.tensor_scalar(ingroup, ingroup, BIG, -BIG, ALU.mult, ALU.add))
                link(ve.tensor_tensor(s4, s4, ingroup.unsqueeze(2).broadcast_to([P, TB * 4, 4]), ALU.add))
                first_best(sel3, key16, by16, ch3, keyed3)
                link(ve.scalar_tensor_tensor(out=sel, in0=chosen, scalar=-BIG, in1=sel, op0=ALU.mult, op1=ALU.add))
                first_best(sel3, key16, by16, hot3, keyed3)
                ve.tensor_tensor(chosen, chosen, hot2, ALU.add).then_inc(s["chosen"], 1)
                dve.wait_ge(s["chosen"], l + 1)
                link(ve.tensor_tensor(sel, score, chosen, ALU.mult))
                link(ve.tensor_reduce(best, sel3, AX, ALU.add))
                link(ve.reciprocal(best, best))
                ve.tensor_tensor(gate3, sel3, best.unsqueeze(2).broadcast_to(by16), ALU.mult)
                rest_of_tokens(2, 1)
                dve.wait_ge(s["ranks"], l + 1)
                link(ve.scalar_tensor_tensor(out=place, in0=R[1][:, 0:2 * E], scalar=1.0, in1=chosen, op0=ALU.add, op1=ALU.mult))
                link(ve.tensor_scalar(place, place, -1.0, None, ALU.add))
                link(ve.tensor_reduce(best[:, 0:1], R[1][:, 2 * E:3 * E], AX, ALU.max))
                steps = const[0:1, C_IOTA + P:C_IOTA + 4 * P].rearrange("p (n m) -> p n m", m=P)[:, :, 0]
                link(ve.tensor_scalar(keyed[0:1, 0:3], steps, best[0:1, 0:1], None, ALU.is_lt))
                link(ve.tensor_reduce(best[0:1, 0:1], keyed[0:1, 0:3], AX, ALU.add))
                ve.tensor_scalar(count[0:1, 0:1], best[0:1, 0:1], float(PAIRS), float(PAIRS), ALU.mult, ALU.add
                                 ).then_inc(s["sweeps_known"], 1)

                def make_onehot(it, twice=False):
                    pair = dve.snap(it % PAIRS)
                    slots = const[:, bass.ds(dve.snap(it // PAIRS * P) + C_IOTA, P if twice else SLOTS)]
                    for b in range(TB):
                        for x in range(2):
                            mine = place[:, bass.ds(pair * 2 + (b * E + x), 1)]
                            if twice:
                                share = gate[:, bass.ds(pair * 2 + (b * E + x), 1)]
                                n = (b * 2 + x) * P
                                m = ve.tensor_scalar(gated[:, n:n + P], slots, mine, share, ALU.is_equal, ALU.mult)
                            else:
                                n = b * P + x * SLOTS
                                m = ve.tensor_scalar(onehot[:, n:n + SLOTS], slots, mine, None, ALU.is_equal)
                    m.then_inc(s["gated_ready" if twice else "onehot_ready"], 1)

                slots = const[:, C_IOTA:C_IOTA + SLOTS]
                for b in range(TB):
                    for x in range(2):
                        n = b * P + x * SLOTS
                        m = ve.tensor_scalar(onehot[:, n:n + SLOTS], slots, place[:, b * E + x:b * E + x + 1], None, ALU.is_equal)
                m.then_inc(s["onehot_ready"], 1)
                rest_of_tokens(3, 3)
                n = iterations(dve, l)
                with dve.Fori(0, n) as it:
                    t = dve.snap(pairs + it)
                    g = dve.snap(t + l)
                    pair_base = dve.snap(t * PAIR + (l + 1) * DENSE)
                    for q in range(PAIR):
                        dve.wait_ge(s["expert_used"], t * PAIR + q + 1)
                        if q == 3:
                            make_onehot(dve.snap(it + 1))
                        rest_of_chunk(q + AHEAD, pair_base)
                        if q == 2:
                            make_onehot(it, twice=True)
                        if 1 <= q <= 4:
                            i = q - 1
                            x4 = slice(i * 512, (i + 1) * 512)
                            dve.wait_ge(s["scattered"], g * 4 + i + 1)
                            ve.tensor_tensor(xT[:, x4], xT[:, x4], DN[i][:], ALU.add).then_inc(s["added"], 1)
                        if q in (5, 7):
                            x = q // 7
                            h = he[:, x * S:(x + 1) * S]
                            h4 = h.rearrange("p (f n) -> p f n", f=4)
                            parts = he_parts[:, x * 512:(x + 1) * 512].rearrange("p (f h n) -> p f h n", f=4, h=2)
                            dve.wait_ge(s["he_silu"], t * 2 + x + 1)
                            ve.tensor_tensor(h, silu[:, x * S:(x + 1) * S], HT[:, S:2 * S], ALU.mult).then_inc(s["pair_link"], 1)
                            dve.wait_ge(s["pair_link"], t * 4 + 2 * x + 1)
                            ve.tensor_copy(parts[:, :, 0, :], h4).then_inc(s["pair_link"], 1)
                            dve.wait_ge(s["pair_link"], t * 4 + 2 * x + 2)
                            rest(parts[:, :, 1, :], h4, parts[:, :, 0, :]).then_inc(s["he_split"], 1)
                dve.reg_add(pairs_done, pairs_done, n)
                steps_done = dve.snap((dve.snap(pairs_done) + l) * 4)
                for i in range(4):
                    x4 = slice(i * 512, (i + 1) * 512)
                    dve.wait_ge(s["scattered"], steps_done + i + 1)
                    ve.tensor_tensor(xT[:, x4], xT[:, x4], DN[i][:], ALU.add).then_inc(s["added"], 1)
                norm(dve.snap(l + 1), 0, V_MIX, link, "plain_ready")
                rest_of_h(dve.snap(l + 1))
                assert n_links[0] == DVE_LINKS, ("DVE_LINKS", n_links[0])


def constants():
    c = np.zeros((P, C_ALL), np.float32)
    i = np.arange(P)
    c[i, C_ID + i] = 1
    c[:, C_ONE:C_ONE + P] = 1
    half = P // 2
    c[np.arange(half) + half, C_SWAP + np.arange(half)] = -1
    c[np.arange(half), C_SWAP + half + np.arange(half)] = 1
    c[:, C_BEFORE:C_BEFORE + P] = i[:, None] < i[None, :]
    gap = np.arange(S)[None, :] - i[:, None]
    for h in range(HEADS):
        log_gamma = np.log(1.0 - 2.0 ** (-5.0 - h))
        c[:, C_DECAY + h * S:C_DECAY + (h + 1) * S] = np.where(gap >= 0, np.exp(np.maximum(gap, 0) * log_gamma) * SCALE, 0.0)
    for n in range(S // SLOTS + 1):
        c[:, C_IOTA + n * P:C_IOTA + (n + 1) * P] = n * SLOTS + i % SLOTS
    c[:, C_EPS] = EPS
    c[i, C_BOTH + i % SLOTS] = 1
    c[:, C_KEY4:C_KEY4 + 4] = 4 - np.arange(4)
    c[:, C_KEY16:C_KEY16 + E] = E - np.arange(E)
    return c


def columns(a):
    a = np.asarray(a)
    return np.moveaxis(a.reshape(*a.shape[:-1], -1, P), -1, 0)


def blocks(w, cols):
    rows = w.shape[0]
    return w.reshape(rows // P, P, -1, cols).transpose(2, 1, 0, 3).reshape(-1, P, rows // P * cols)


def chunks(w, cols):
    return blocks(np.asarray(w), cols)


def kernel(x, mem, positions, norm_mix_g, w_in, b_branch_gate, ret_norm_g, w_ret_out, conv_w, conv_b, conv_ln_g,
           conv_ln_b, w_conv_out, w_mix_out, norm_xattn_g, norm_mem_g, w_xq, w_xkv, w_xo, norm_ffn_g, w_router,
           b_router, w_exp_gate, w_exp_up, w_exp_down, norm_final_g):
    import concourse.bacc as bacc
    from concourse.bass_utils import run_bass_kernel_spmd

    depth = w_in.shape[0]
    vec = np.zeros((P, depth + 1, V_ALL), np.float32)
    for at, a in ((V_MIX, norm_mix_g), (V_XATTN, norm_xattn_g), (V_MEM, norm_mem_g), (V_FFN, norm_ffn_g),
                  (V_BG, b_branch_gate), (V_RET, ret_norm_g), (V_CB, conv_b), (V_LG, conv_ln_g), (V_LB, conv_ln_b)):
        a = columns(a)
        vec[:, :depth, at:at + a.shape[2]] = a
    vec[:, depth, V_MIX:V_MIX + KD] = columns(norm_final_g)
    vec[:, :depth, V_TAP:] = columns(conv_w).reshape(P, depth, TAPS * CB)
    glob = np.zeros((P, G_ALL), np.float32)
    glob[:, G_RT:G_RT + KD * E] = np.asarray(w_router).reshape(KD, P, E).transpose(1, 0, 2).reshape(P, -1)
    glob[:, G_BR:G_BR + E] = np.asarray(b_router)[None, :]
    glob[:, G_FREQ] = np.float32(10000.0) ** (-(np.arange(P) % (P // 2)).astype(np.float32) / (P // 2))
    dense = np.empty((depth, DENSE, P, CHUNK), np.float32)
    experts = np.empty((depth * PAIRS, PAIR, P, CHUNK), np.float32)
    for l in range(depth):
        win = chunks(w_in[l], 256).reshape(10, 2, P, CHUNK)
        for at, n, m in ((CH_Q, 0, 1), (CH_K, 1, 1), (CH_V, 2, 1), (CH_SG, 3, 1), (CH_CA, 4, 1), (CH_CG, 5, 1), (CH_G, 6, 4)):
            dense[l, at:at + 2 * m] = win[n:n + m].reshape(-1, P, CHUNK)
        xkv = chunks(w_xkv[l], 256)
        for at, w in ((CH_RET, chunks(w_ret_out[l], 512)), (CH_CONV, chunks(w_conv_out[l], 512)), (CH_MIX, chunks(w_mix_out[l], 256)),
                      (CH_XQ, chunks(w_xq[l], 256)), (CH_XO, chunks(w_xo[l], 512))):
            dense[l, at:at + len(w)] = w
        for at, w in zip(CH_XK + CH_XV, xkv):
            dense[l, at] = w
        for e in range(E):
            pair, second = l * PAIRS + e // 2, e % 2
            for at, w, cols in ((4 * second, w_exp_gate, 512), (4 * second + 2, w_exp_up, 512),
                                (8 + 2 * second, w_exp_down, D)):
                unit = chunks(w[l, e], cols)[0]
                experts[pair, at], experts[pair, at + 1] = unit[:, :CHUNK], unit[:, CHUNK:]

    def turned(a):
        return np.ascontiguousarray(np.asarray(a)[0].T.reshape(KD, P, S).transpose(1, 0, 2))

    arrays = {
        "x_in": turned(x), "mem_in": turned(mem),
        "positions_in": np.ascontiguousarray(np.broadcast_to(np.asarray(positions)[None, :], (P, S))),
        "constants_in": constants(), "vectors_in": vec.reshape(P, -1), "globals_in": glob,
        "dense_in": dense, "experts_in": experts,
    }
    nc = bacc.Bacc("TRN2", target_bir_lowering=False, num_devices=1)
    args = [nc.dram_tensor(n, a.shape, mybir.dt.from_np(a.dtype), kind="ExternalInput").ap() for n, a in arrays.items()]
    out = nc.dram_tensor("out", (P, KD, S), F32, kind="ExternalOutput").ap()
    build(nc, *args, out)
    got = run_bass_kernel_spmd(nc, [arrays], core_ids=[0]).results[0]["out"]
    return np.ascontiguousarray(got.transpose(2, 1, 0).reshape(1, S, D))
```

```python
from contextlib import ExitStack

import numpy as np
import concourse.bass as bass
from concourse import mybir

P = 128
D = 1024
S = 256
KD = D // P
TB = S // P
HEADS = 4
CB = 4
TAPS = 31
ZW = S + TAPS - 1
E = 16
SLOTS = 64
PAIRS = E // 2
UNROLL = 2
STEPS = PAIRS // UNROLL
CHUNK = 2048
RAW = 4
SPLIT = 4
DENSE = 36
PAIR = 12
AHEAD = SPLIT
EPS = 1e-6
SCALE = float(P) ** -0.5
BIG = 1e30
TWO_PI = 2.0 * np.pi
PI_A = 6.28125
PI_B = float(np.float32(np.floor((TWO_PI - PI_A) * 2.0 ** 20) / 2.0 ** 20))
PI_C = float(TWO_PI - PI_A - PI_B)
MAGIC = 12582912.0

C_ID, C_ONE, C_SWAP, C_BEFORE = 0, 128, 256, 384
C_BAND = 512
C_IOTA = C_BAND + 7 * 32
C_KEY4 = C_IOTA + (S // SLOTS + 1) * P
C_KEY16 = C_KEY4 + 4
C_EPS = C_KEY16 + 16
C_BOTH = C_EPS + 1
C_DECAY = C_BOTH + SLOTS
C_ALL = C_DECAY + HEADS * S

V_MIX, V_XATTN, V_MEM, V_FFN = 0, 8, 16, 24
V_BG = 32
V_RET = 48
V_CB, V_LG, V_LB = 52, 56, 60
V_TAP = 64
V_ALL = V_TAP + TAPS * CB

G_RT, G_BR, G_FREQ = 0, 128, 144
G_ALL = G_RT + (KD - 1) * E + P

F32 = mybir.dt.float32
F32R = mybir.dt.float32r
I32 = mybir.dt.int32
ALU = mybir.AluOpType
ACT = mybir.ActivationFunctionType
AX = mybir.AxisListType.X

DVE_LINKS = 46

(CH_CG, CH_CA, CH_Q, CH_K, CH_V, CH_SG, CH_G, CH_RET, CH_CONV, CH_MIX, CH_XQ, CH_XO) = (
    0, 2, 4, 6, 8, 10, 12, 21, 23, 26, 31, 34)
CH_XK, CH_XV = (20, 25), (30, 33)
JOBS_OF_CHUNK = [2 if CH_RET <= c < CH_XK[1] or c >= CH_XO else 1 for c in range(DENSE)]
JOB = [sum(JOBS_OF_CHUNK[:c]) for c in range(DENSE + 1)]
JOBS = JOB[DENSE]
RB = 4
JOBS_OF_BANK = [len(range(b, JOBS, RB)) for b in range(RB)]

H_H, H_MEMN, H_R, H_CZ, H_MIX, H_H2, H_O = 0, 4, 6, 7, 8, 10, 14
PIECES = 16
PLAIN = PIECES - 2

TAP_ORDER = [(w, k) for pair in ((0, 1), (2, 3)) for w in range(TAPS) for k in pair]
TAP_STEPS = [4] * 2 + [12] * 3 + [8] * 4 + [8] * 6


def build(nc, xT_d, memT_d, pos_d, const_d, vec_d, glob_d, dense_d, experts_d, out_d):
    depth = dense_d.shape[0]
    ctx = ExitStack()
    with ctx:
        def sb(name, cols, dt=F32, rows=P):
            return ctx.enter_context(nc.sbuf_tensor(name, [rows, cols], dt))

        def sem(name):
            return ctx.enter_context(nc.semaphore(name))

        raw = sb("raw", RAW * CHUNK)
        whi = sb("whi", SPLIT * CHUNK, F32R)
        wlo = sb("wlo", SPLIT * CHUNK, F32R)
        a_hi, a_lo = sb("a_hi", KD * S, F32R), sb("a_lo", KD * S, F32R)
        b_hi, b_lo = sb("b_hi", KD * S, F32R), sb("b_lo", KD * S, F32R)
        const = sb("const", C_ALL)
        vec = sb("vec", (depth + 1) * V_ALL)
        glob = sb("glob", G_ALL)
        sin, cos = sb("sin", S), sb("cos", S)
        xT = sb("xT", KD * S)
        gates = sb("gates", 16 * S)
        qk = sb("qk", 2 * HEADS * S)
        v = sb("v", TB * 512)
        sg = sb("sg", HEADS * S)
        zp = sb("zp", CB * ZW)
        cz = sb("cz", CB * S)
        r = sb("r", HEADS * S)
        tmp = sb("tmp", KD * S)
        rstd = sb("rstd", S)
        rmem = sb("rmem", S)
        small = sb("small", 256)
        count = sb("count", 1, I32, 1)
        pos_i = gates[:, 0:S].bitcast(I32)

        sT = tmp[:, 0:HEADS * 384]
        mixin = qk
        qx = sg
        kx = v
        vx = zp
        probs = gates[:, 0:2048]
        pT = gates[:, 2048:4096]
        r_rms = tmp[:, 1024:1024 + S]
        gated = gates[:, 0:512]
        gatedT = gates[:, 512:1024]
        ye = gates[:, 1024:3072]
        gu = gates[:, 3072:4096]
        silu = cz
        he = r
        xg = b_hi
        onehot = b_lo[:, 0:S]
        he_parts = b_lo[:, S:S + 1024]

        ps = [ctx.enter_context(nc.psum_tensor(f"bank{i}", [P, 512], F32)) for i in range(8)]
        R, M = ps[0:4], ps[4:8]
        GATE, UP, HT, GB = ps[0:4]
        DN = ps[4:8]
        GATHER_BANKS = (GB, GATE, UP, GB)

        ident = const[:, C_ID:C_ID + P]
        ones = const[:, C_ONE:C_ONE + P]
        swap = const[:, C_SWAP:C_SWAP + P]
        before = const[:, C_BEFORE:C_BEFORE + P]
        eps = const[:, C_EPS:C_EPS + 1]
        both = const[:, C_BOTH:C_BOTH + SLOTS]

        names = """const_in decay_in pos_in x_in mem_in out_sent hi_done split_done
            mem_squares mem_sum mem_root angle sin_done
            squares norm_sum norm_root normed plain_ready part_hi part_split
            proj_done qk_raw swapped rotated scores masked r_sum r_squares r_norm_sum r_root r_inverse r_factor
            z_made conv_tap ln_mean ln_centred ln_squares ln_var ln_root ln_scaled
            att_scores att_max att_exp att_probs att_T att_pT att_o
            logits router_sig score_turned tok_T tok_hi tok_split chosen ranks sweeps_known count_due
            expert_used zeroed onehot_ready gated_ready gathered xg_ready gate_copied up_copied turned silu_table he_silu
            he_split gatedT_psum gatedT_ready y_copied scattered added pair_link
            link start_link""".split()
        s = {n: sem(n) for n in names}
        landed = [sem(f"landed{i}") for i in range(RAW)]
        bank_free = [sem(f"bank_free{i}") for i in range(RB)]

        at = [0]

        def part_of_small(n):
            at[0] += n
            return small[:, at[0] - n:at[0]]

        chosen, softmax, gate, place = (part_of_small(TB * E) for _ in range(4))
        score3 = R[2][:, 0:S].rearrange("p (b e) -> p b e", b=TB)[:, :, 0:E]
        scores_T = sg[:, 0:S]
        sel, keyed = part_of_small(TB * E), part_of_small(TB * E)
        sums, group, ingroup, best = part_of_small(32), part_of_small(8), part_of_small(8), part_of_small(2)
        neg_max, exp_sum = softmax[:, 0:8], softmax[:, 8:16]
        hot2 = place
        table_out = part_of_small(1)

        block = ctx.enter_context(nc.Block())

        def vcol(l, col):
            return vec[:, bass.ds(l * V_ALL + col, 1)]

        def raw_chunk(c):
            return raw[:, (c % RAW) * CHUNK:(c % RAW + 1) * CHUNK]

        def part(w, c):
            return w[:, (c % SPLIT) * CHUNK:(c % SPLIT + 1) * CHUNK]

        def iterations(eng, l):
            eng.wait_ge(s["sweeps_known"], l + 1)
            eng.sem_inc(s["count_due"], 1)
            return eng.value_load(count[0:1, 0:1], min_val=STEPS, max_val=STEPS * (S // SLOTS))

        def add_pairs(eng, pairs_done, n):
            for _ in range(UNROLL):
                eng.reg_add(pairs_done, pairs_done, n)

        def counter(eng):
            pairs_done = eng.alloc_register("pairs_done")
            eng.reg_mov(pairs_done, 0)
            return pairs_done

        def freed(eng, l, j):
            eng.wait_ge(bank_free[j % RB], l * JOBS_OF_BANK[j % RB] + j // RB + 1)

        @block.sync
        def _(sp):
            def load(c, src, base=None):
                if base is not None:
                    sp.wait_ge(s["split_done"], base + c + 1)
                sp.dma_start(raw_chunk(c), src.rearrange("o p n -> p (o n)")).then_inc(landed[c % RAW], 16)

            sp.dma_start(xT[:].rearrange("p (k t) -> p k t", k=KD), xT_d).then_inc(s["x_in"], 16)
            sp.dma_start(glob[:], glob_d).then_inc(s["pos_in"], 16)
            sp.dma_start(pos_i, pos_d).then_inc(s["pos_in"], 16)
            sp.dma_start(const[:, :C_DECAY], const_d[:, :C_DECAY]).then_inc(s["const_in"], 16)
            sp.dma_start(vec[:], vec_d).then_inc(s["const_in"], 16)
            load(0, dense_d[0:1, 0])
            sp.dma_start(qk[:].rearrange("p (k t) -> p k t", k=KD), memT_d).then_inc(s["mem_in"], 16)
            for c in range(1, AHEAD):
                load(c, dense_d[0:1, c])
            sp.dma_start(const[:, C_DECAY:], const_d[:, C_DECAY:]).then_inc(s["decay_in"], 16)
            sp.sem_inc(s["split_done"], RAW)
            pairs_done = counter(sp)
            with sp.Fori(0, depth) as l:
                pairs = sp.snap(pairs_done)
                base = sp.snap(l * DENSE + pairs * PAIR)
                for c in range(AHEAD, DENSE):
                    load(c, dense_d[bass.ds(l, 1), c], base)
                for x in range(UNROLL):
                    for q in range(PAIR):
                        load(DENSE + x * PAIR + q, experts_d[bass.ds(l * PAIRS + x, 1), q], base)
                n = iterations(sp, l)
                with sp.Fori(1, n) as step:
                    loop_base = sp.snap(base + (step * (UNROLL * PAIR) + DENSE))
                    for x in range(UNROLL):
                        for q in range(PAIR):
                            load(x * PAIR + q, experts_d[bass.ds(l * PAIRS + step % STEPS * UNROLL + x, 1), q], loop_base)
                add_pairs(sp, pairs_done, n)
                next_base = sp.snap((l + 1) * DENSE + sp.snap(pairs_done) * PAIR)
                for c in range(AHEAD):
                    load(c, dense_d[bass.ds((l + 1) % depth, 1), c], next_base)
                sp.wait_ge(s["normed"], l * 4 + 4)
                sp.dma_start(qk[:].rearrange("p (k t) -> p k t", k=KD), memT_d).then_inc(s["mem_in"], 16)
            sp.wait_ge(s["mem_in"], (depth + 1) * 16)
            for i in range(4):
                sp.wait_ge(s["plain_ready"], depth * PLAIN + i + 1)
                sp.dma_start(out_d[:, 2 * i:2 * i + 2], tmp[:, i * 512:(i + 1) * 512].rearrange("p (k t) -> p k t", k=2)
                             ).then_inc(s["out_sent"], 16)
            sp.wait_ge(s["out_sent"], 64)

        @block.tensor
        def _(pe):
            mm = nc.tensor.matmul

            def column_sum(out, squares, blocks):
                for k in range(blocks):
                    m = mm(out, ones, squares[:, k * S:(k + 1) * S], start=k == 0, stop=k == blocks - 1)
                return m

            def norm_sum(out, n, quarters=range(4)):
                for i in quarters:
                    pe.wait_ge(s["squares"], n * 4 + i + 1)
                    mm(out, ones, tmp[:, 2 * i * S:(2 * i + 1) * S], start=i == 0, stop=False)
                    m = mm(out, ones, tmp[:, (2 * i + 1) * S:(2 * i + 2) * S], start=False, stop=i == 3)
                    if i == 3:
                        m.then_inc(s["norm_sum"], 1)

            def keep_clock(n):
                for _ in range(n):
                    mm(GB[:, 0:S], ones, const[:, 0:S], start=True, stop=True)

            pe.wait_ge(s["const_in"], 32)
            norm_sum(HT[:, 0:S], 0)
            pe.wait_ge(s["mem_squares"], 1)
            column_sum(M[2][:, 0:S], gates[:, 2048:4096], KD).then_inc(s["mem_sum"], 1)
            pairs_done = counter(pe)
            with pe.Fori(0, depth) as l:
                pairs = pe.snap(pairs_done)
                base = pe.snap(l * DENSE + pairs * PAIR + RAW)

                def weights(c, chunk_base=base):
                    pe.wait_ge(s["split_done"], chunk_base + c + 1)
                    return part(whi, c), part(wlo, c)

                def bank(j):
                    if j >= RB:
                        freed(pe, l, j - RB)
                    return R[j % RB]

                def piece(i):
                    pe.wait_ge(s["part_split"], l * PIECES + i + 1)

                def project(c, src, piece0, blocks, rows, first=0):
                    hi, lo = weights(c)
                    for b in range(blocks):
                        j = JOB[c] + b // 2
                        out = (bank(j) if b % 2 == 0 else R[j % RB])[:, (b % 2) * S:(b % 2 + 1) * S]
                        for k in range(rows):
                            if first and b == 0 and k % (rows // first) == 0:
                                piece(piece0 + k // (rows // first))
                            w = slice((k * blocks + b) * P, (k * blocks + b + 1) * P)
                            x = slice(k * S, (k + 1) * S)
                            mm(out, hi[:, w], src[0][:, x], start=k == 0, stop=False)
                            mm(out, hi[:, w], src[1][:, x], start=False, stop=False)
                            m = mm(out, lo[:, w], src[0][:, x], start=False, stop=k == rows - 1)
                        if b % 2 == 1:
                            m.then_inc(s["proj_done"], 1)

                def project_values(c, src):
                    hi, lo = weights(c)
                    out = bank(JOB[c])
                    for b in range(TB):
                        o = out[:, b * S:(b + 1) * S]
                        for k in range(KD):
                            x = slice(k * S + b * P, k * S + b * P + P)
                            w = slice(k * S, (k + 1) * S)
                            mm(o, src[0][:, x], hi[:, w], start=k == 0, stop=False)
                            mm(o, src[1][:, x], hi[:, w], start=False, stop=False)
                            m = mm(o, src[0][:, x], lo[:, w], start=False, stop=k == KD - 1)
                    m.then_inc(s["proj_done"], 1)

                A, B = (a_hi, a_lo), (b_hi, b_lo)
                rc = (a_hi[:, 1024:2048], a_lo[:, 1024:2048])
                for c in range(DENSE):
                    if c in (CH_V, CH_V + 1):
                        project_values(c, A)
                    elif c in CH_XV:
                        project_values(c, B)
                    elif c in CH_XK:
                        project(c, B, H_MEMN, 2, KD, first=2 * (c == CH_XK[0]))
                    elif c < CH_RET:
                        project(c, A, H_H, 2, KD, first=4 * (c == 0))
                    elif c < CH_CONV:
                        project(c, A, H_R, 4, CB, first=c == CH_RET)
                    elif c < CH_MIX:
                        project(c, rc, H_CZ, 4, CB, first=c == CH_CONV)
                    elif c < CH_XQ:
                        project(c, A, H_MIX, 2, KD, first=2 * (c == CH_MIX))
                    elif c < CH_XO:
                        project(c, A, H_H2, 2, KD, first=4 * (c == CH_XQ))
                    else:
                        project(c, A, H_O, 4, CB, first=2 * (c == CH_XO))

                    if CH_K <= c < CH_K + 4:
                        i = c - CH_K
                        pe.wait_ge(s["qk_raw"], l * 4 + i + 1)
                        mm(M[i][:], swap, qk[:, i * 512:(i + 1) * 512], start=True, stop=True).then_inc(s["swapped"], 1)
                    if c == 12:
                        pe.wait_ge(s["rotated"], l * 4 + 4)
                        for h in range(HEADS):
                            q = qk[:, h * S:(h + 1) * S]
                            k = qk[:, (HEADS + h) * S:(HEADS + h + 1) * S]
                            mm(M[h][:, 0:S], k[:, 0:P], q, start=True, stop=True)
                            mm(M[h][:, S:S + P], k[:, P:S], q[:, P:S], start=True, stop=True).then_inc(s["scores"], 1)
                    if c == 15:
                        pe.wait_ge(s["masked"], l * HEADS + HEADS)
                        for h in range(HEADS):
                            out = M[h // 2][:, (h % 2) * S:(h % 2 + 1) * S]
                            mm(out, v[:, h * P:(h + 1) * P], sT[:, h * 384:h * 384 + S], start=True, stop=False)
                            mm(out[:, P:S], v[:, 512 + h * P:512 + (h + 1) * P], sT[:, h * 384 + S:h * 384 + 384],
                               start=False, stop=True).then_inc(s["r_sum"], 1)
                    if c == 16:
                        for h in range(HEADS):
                            if h % 2 == 0:
                                pe.wait_ge(s["r_squares"], l * 2 + h // 2 + 1)
                            m = mm(M[2][:, 0:S], const[:, C_BAND + (3 - h) * 32:C_BAND + (3 - h) * 32 + P], tmp[:, h * S:(h + 1) * S],
                                   start=h == 0, stop=h == HEADS - 1)
                        m.then_inc(s["r_norm_sum"], 1)
                    if c == 18:
                        pe.wait_ge(s["conv_tap"], (l + 1) * (TAPS * CB))
                        column_sum(M[0][:, 0:S], cz, CB).then_inc(s["ln_mean"], 1)
                        pe.wait_ge(s["r_inverse"], l + 1)
                        for h in range(HEADS):
                            m = mm(M[2 + h // 2][:, (h % 2) * S:(h % 2 + 1) * S], ident[:, 32 * h:32 * h + 1].broadcast_to([P, P]),
                                   r_rms, start=True, stop=True)
                        m.then_inc(s["r_factor"], 1)
                    if c == 19:
                        pe.wait_ge(s["ln_squares"], l + 1)
                        column_sum(M[1][:, 0:S], tmp, CB).then_inc(s["ln_var"], 1)
                    if CH_MIX < c <= CH_MIX + 3:
                        norm_sum(M[2][:, 0:S], l * 3 + 1, (c - CH_MIX - 1,) if c < CH_MIX + 3 else (2, 3))
                    if c == CH_XO + 1:
                        norm_sum(M[2][:, 0:S], l * 3 + 2, (0, 1))
                    if c == CH_XQ + 1:
                        freed(pe, l, JOB[CH_XQ])
                        freed(pe, l, JOB[CH_XQ] + 1)
                        for h in range(HEADS):
                            for b in range(TB):
                                m = mm(M[h][:, b * S:(b + 1) * S], qx[:, h * S + b * P:h * S + b * P + P],
                                       kx[:, h * S:(h + 1) * S], start=True, stop=True)
                            m.then_inc(s["att_scores"], 1)
                    if c == CH_XV[1]:
                        for h in range(HEADS):
                            pe.wait_ge(s["att_probs"], l * HEADS + h + 1)
                            for k in range(TB):
                                for b in range(TB):
                                    p = (h * TB + b) * S + k * P
                                    m = nc.tensor.transpose(M[h][:, k * S + b * P:k * S + b * P + P], probs[:, p:p + P], ident)
                            m.then_inc(s["att_T"], 1)
                        freed(pe, l, JOB[CH_XV[1]])
                        for h in range(HEADS):
                            pe.wait_ge(s["att_pT"], l * HEADS + h + 1)
                            for k in range(TB):
                                m = mm(M[h // 2][:, (h % 2) * S:(h % 2 + 1) * S],
                                       vx[:, (h // 2) * 512 + k * S + (h % 2) * P:(h // 2) * 512 + k * S + (h % 2) * P + P],
                                       pT[:, (h * TB + k) * S:(h * TB + k + 1) * S], start=k == 0, stop=k == TB - 1)
                            m.then_inc(s["att_o"], 1)

                norm_sum(M[2][:, 0:S], l * 3 + 2, (2, 3))

                def logits(half_of_features):
                    for k in range(half_of_features * 4, half_of_features * 4 + 4):
                        m = mm(R[0][:, 0:S], glob[:, G_RT + k * E:G_RT + k * E + P], tmp[:, k * S:(k + 1) * S],
                               start=k == 0, stop=k == KD - 1)
                    return m

                def turn_tokens(half_of_features):
                    for b in range(TB):
                        for q in range(4):
                            k = half_of_features * 4 + q
                            m = nc.tensor.transpose(M[2 * b + half_of_features][:, q * P:(q + 1) * P],
                                                    tmp[:, k * S + b * P:k * S + b * P + P], ident)
                        m.then_inc(s["tok_T"], 1)

                keep_clock(8)
                pe.wait_ge(s["normed"], l * 4 + 2)
                logits(0)
                turn_tokens(0)
                pe.wait_ge(s["normed"], l * 4 + 4)
                logits(1).then_inc(s["logits"], 1)
                turn_tokens(1)
                pe.wait_ge(s["router_sig"], l + 1)
                for b in range(TB):
                    m = nc.tensor.transpose(R[2][:, b * P:(b + 1) * P], scores_T[:, b * P:(b + 1) * P], ident)
                m.then_inc(s["score_turned"], 1)
                keep_clock(12)
                pe.wait_ge(s["chosen"], l + 1)
                mm(R[1][:, 0:2 * E], before, chosen, start=True, stop=False)
                mm(R[1][:, E:2 * E], ones, chosen[:, 0:E], start=False, stop=True)
                mm(R[1][:, 2 * E:3 * E], ones, chosen[:, 0:E], start=True, stop=False)
                mm(R[1][:, 2 * E:3 * E], ones, chosen[:, E:2 * E], start=False, stop=True).then_inc(s["ranks"], 1)

                def gather(i, out):
                    src = a_hi if i < 2 else a_lo
                    for k in range(4):
                        f = (i % 2) * 4 + k
                        for b in range(TB):
                            m = mm(out[:, k * P:(k + 1) * P], src[:, b * D + f * P:b * D + (f + 1) * P],
                                   onehot[:, b * P:(b + 1) * P], start=b == 0, stop=b == TB - 1)
                    m.then_inc(s["gathered"], 1)

                def scatter(i):
                    for k in range(2):
                        f = (2 * i + k) * P
                        for x in range(2):
                            m = mm(DN[i][:, k * S:(k + 1) * S], ye[:, x * D + f:x * D + f + P],
                                   gatedT[:, x * S:(x + 1) * S], start=x == 0, stop=x == 1)
                    m.then_inc(s["scattered"], 1)

                pe.wait_ge(s["zeroed"], l + 1)
                gathers = pe.snap(l + pairs)
                pe.wait_ge(s["onehot_ready"], gathers + 1)
                pe.wait_ge(s["tok_hi"], l * 4 + 4)
                for i in range(4):
                    if i == 2:
                        pe.wait_ge(s["tok_split"], l * 4 + 4)
                    if i == 3:
                        pe.wait_ge(s["xg_ready"], gathers * 4 + 1)
                    gather(i, GATHER_BANKS[i])

                n = iterations(pe, l)
                with pe.Fori(0, n) as step:
                    for of_step in range(UNROLL):
                        it = pe.snap(step * UNROLL + of_step)
                        t = pe.snap(it + pairs)
                        g = pe.snap(t + l)
                        pair_base = pe.snap(t * PAIR + (l + 1) * DENSE + RAW)
                        pe.wait_ge(s["xg_ready"], g * 4 + 4)
                        for q in range(PAIR):
                            hi, lo = weights(q, pair_base)
                            if q < 8:
                                x, up, c = q // 4, q % 4 // 2, q % 2
                                if q == 4:
                                    pe.wait_ge(s["gate_copied"], t * 2 + 1)
                                if q == 6:
                                    pe.wait_ge(s["up_copied"], t * 2 + 1)
                                for k in range(4):
                                    tok = xg[:, x * D + (c * 4 + k) * P:x * D + (c * 4 + k + 1) * P]
                                    mm((GATE, UP)[up][:], tok, hi[:, k * 512:(k + 1) * 512], start=c == 0 and k == 0, stop=False)
                                    m = mm((GATE, UP)[up][:], tok, lo[:, k * 512:(k + 1) * 512], start=False, stop=c == 1 and k == 3)
                            else:
                                x, c = (q - 8) // 2, q % 2
                                if c == 0:
                                    pe.wait_ge(s["he_split"], t * 2 + x + 1)
                                    if x == 0:
                                        pe.wait_ge(s["added"], g * 4 + 4)
                                for k in range(2):
                                    rows = he_parts[:, x * 512 + (c * 2 + k) * P:x * 512 + (c * 2 + k + 1) * P]
                                    for o in range(2):
                                        w = slice(k * D + o * 512, k * D + (o + 1) * 512)
                                        mm(DN[2 * x + o][:], rows, hi[:, w], start=c == 0 and k == 0, stop=False)
                                        m = mm(DN[2 * x + o][:], rows, lo[:, w], start=False, stop=c == 1 and k == 1)
                            m.then_inc(s["expert_used"], 1)
                            if 1 <= q <= 4:
                                if q == 1:
                                    pe.wait_ge(s["y_copied"], t * 4 + 4 * (l + 1))
                                scatter(q - 1)
                            if q == 7:
                                pe.wait_ge(s["gatedT_ready"], t + 1)
                                pe.wait_ge(s["onehot_ready"], g + 2)
                                gather(0, GATHER_BANKS[0])
                            if q in (5, 7):
                                x = q // 7
                                pe.wait_ge(s["gate_copied"], t * 2 + x + 1)
                                pe.wait_ge(s["up_copied"], t * 2 + x + 1)
                                if x == 1:
                                    pe.wait_ge(s["he_split"], t * 2 + 1)
                                for f in range(8):
                                    m = mm(HT[:, f * SLOTS:(f + 1) * SLOTS], gu[:, f * P:(f + 1) * P], both, start=True, stop=True)
                                m.then_inc(s["turned"], 1)
                            if q == 5:
                                pe.wait_ge(s["gated_ready"], t + 1)
                                for x in range(2):
                                    for b in range(TB):
                                        m = nc.tensor.transpose(GB[:, x * S + b * P:x * S + b * P + P],
                                                                gated[:, (b * 2 + x) * P:(b * 2 + x + 1) * P], ident)
                                m.then_inc(s["gatedT_psum"], 1)
                            if q == 8:
                                gather(1, GATHER_BANKS[1])
                                gather(2, GATHER_BANKS[2])
                            if q == 9:
                                pe.wait_ge(s["xg_ready"], g * 4 + 5)
                                gather(3, GATHER_BANKS[3])
                add_pairs(pe, pairs_done, n)
                after = pe.snap(pairs_done)
                pe.wait_ge(s["y_copied"], after * 4 + 4 * (l + 1))
                for i in range(4):
                    scatter(i)
                norm_sum(HT[:, 0:S], l * 3 + 3)
                pe.wait_ge(s["xg_ready"], pe.snap((after + l + 1) * 4))
                keep_clock(8)

        @block.scalar
        def _(act):
            activate = nc.scalar.activation

            def copy(out, src):
                return activate(out, src, ACT.Copy)

            def square(i):
                q = slice(i * 512, (i + 1) * 512)
                activate(tmp[:, q], xT[:, q], ACT.Square, scale=D ** -0.5).then_inc(s["squares"], 1)

            def root(out, mean, scale=1.0):
                return activate(out, mean, ACT.Sqrt, bias=eps, scale=scale)

            def norm_root(l, n, bank):
                act.wait_ge(s["norm_sum"], l * 3 + n + 1)
                root(rstd[:], bank[:, 0:S]).then_inc(s["norm_root"], 1)

            def round_piece(l, i, dst, src):
                act.wait_ge(s["plain_ready"], l * PLAIN + i + 1)
                copy(dst, src).then_inc(s["part_hi"], 1)

            def round_h(l):
                for i in range(4):
                    h = slice(i * 512, (i + 1) * 512)
                    round_piece(l, H_H + i, a_hi[:, h], tmp[:, h])

            act.wait_ge(s["x_in"], 16)
            for i in range(4):
                square(i)
            act.wait_ge(landed[0], 16)
            copy(part(whi, 0), raw_chunk(0)).then_inc(s["hi_done"], 1)
            act.wait_ge(s["const_in"], 32)
            norm_root(0, 0, HT)
            act.wait_ge(s["mem_in"], 16)
            activate(gates[:, 2048:4096], qk[:], ACT.Square, scale=D ** -0.5).then_inc(s["mem_squares"], 1)
            round_h(0)
            for c in range(1, AHEAD):
                act.wait_ge(landed[c], 16)
                copy(part(whi, c), raw_chunk(c)).then_inc(s["hi_done"], 1)
            act.wait_ge(s["mem_sum"], 1)
            root(rmem[:], M[2][:, 0:S]).then_inc(s["mem_root"], 1)
            act.wait_ge(s["angle"], 1)
            activate(sin[:], gates[:, 256:512], ACT.Sin)
            activate(cos[:], gates[:, 512:768], ACT.Sin).then_inc(s["sin_done"], 1)
            pairs_done = counter(act)
            with act.Fori(0, depth) as l:
                pairs = act.snap(pairs_done)
                rounds = act.snap(l * (DENSE // RAW) + pairs * (PAIR // RAW))

                def round_chunk(c, from_round):
                    act.wait_ge(landed[c % RAW], (from_round + c // RAW + 1) * 16)
                    copy(part(whi, c), raw_chunk(c)).then_inc(s["hi_done"], 1)

                for c in range(AHEAD, DENSE + AHEAD):
                    u = c - AHEAD
                    act.wait_ge(s["proj_done"], l * JOBS + JOB[u + 1])
                    src = R[JOB[u] % RB]
                    free = bank_free[JOB[u] % RB]
                    if u < CH_CA:
                        activate(sg[:, u * 512:(u + 1) * 512], src[:], ACT.Sigmoid).then_inc(free, 1)
                    if u in (1, 2):
                        i = u - 1
                        round_piece(l, H_MEMN + i, b_hi[:, i * 1024:(i + 1) * 1024], qk[:, i * 1024:(i + 1) * 1024])
                    if CH_Q <= u < CH_V:
                        i = u - CH_Q
                        if i == 0:
                            act.wait_ge(s["part_split"], l * PIECES + H_MEMN + 2)
                        copy(qk[:, i * 512:(i + 1) * 512], src[:]).then_inc(s["qk_raw"], 1)
                        act.wait_ge(s["qk_raw"], l * 4 + i + 1)
                        act.sem_inc(free, 1)
                    if CH_V <= u < CH_SG:
                        i = u - CH_V
                        copy(v[:].rearrange("p (b n) -> p b n", b=TB)[:, :, i * S:(i + 1) * S],
                             src[:].rearrange("p (b n) -> p b n", b=TB)).then_inc(free, 1)
                    if CH_SG <= u < CH_G:
                        i = u - CH_SG
                        if i == 0:
                            act.wait_ge(s["z_made"], l * 2 + 2)
                        activate(sg[:, i * 512:(i + 1) * 512], src[:], ACT.Silu).then_inc(free, 1)
                    if CH_G <= u < CH_XK[0]:
                        i = u - CH_G
                        for k in range(2):
                            f = 2 * i + k
                            m = activate(gates[:, f * S:(f + 1) * S], src[:, k * S:(k + 1) * S], ACT.Sigmoid,
                                         bias=vcol(l, V_BG + f))
                        m.then_inc(free, 1)
                    if u in CH_XK:
                        i = CH_XK.index(u)
                        copy(kx[:, i * 512:(i + 1) * 512], src[:]).then_inc(free, 1)
                    if u in CH_XV:
                        i = CH_XV.index(u)
                        copy(vx[:, i * 512:(i + 1) * 512], src[:]).then_inc(free, 1)
                    if CH_XQ <= u < CH_XO and u not in CH_XV:
                        i = u - CH_XQ
                        copy(qx[:, i * 512:(i + 1) * 512], src[:]).then_inc(free, 1)
                    if CH_MIX <= u < CH_MIX + 4:
                        freed(act, l, JOB[u])
                        square(u - CH_MIX)
                    if u >= CH_XO:
                        for j in (JOB[u], JOB[u] + 1):
                            freed(act, l, j)
                            square(j - JOB[CH_XO])
                    if u == CH_MIX + 3:
                        norm_root(l, 1, M[2])
                    if u == DENSE - 1:
                        norm_root(l, 2, M[2])
                    round_chunk(c, rounds)
                    if u == 15:
                        for i in range(2):
                            act.wait_ge(s["r_sum"], l * HEADS + 2 * i + 2)
                            h = slice(i * 512, (i + 1) * 512)
                            copy(r[:, h], M[i][:])
                            activate(tmp[:, h], M[i][:], ACT.Square, scale=(2 * P) ** -0.5).then_inc(s["r_squares"], 1)
                    if u == 16:
                        act.wait_ge(s["r_norm_sum"], l + 1)
                        root(r_rms, M[2][:, 0:S], 2.0).then_inc(s["r_root"], 1)
                    if u == 18:
                        act.wait_ge(s["ln_centred"], l + 1)
                        activate(tmp[:, 0:1024], cz[:], ACT.Square, scale=(2 * CB * P) ** -0.5).then_inc(s["ln_squares"], 1)
                    if u == 19:
                        act.wait_ge(s["ln_var"], l + 1)
                        root(rstd[:], M[1][:, 0:S], 2.0).then_inc(s["ln_root"], 1)
                        round_piece(l, H_R, a_hi[:, 0:1024], r[:])
                    if u == 20:
                        act.wait_ge(s["ln_scaled"], l + 1)
                        for k in range(CB):
                            blk = cz[:, k * S:(k + 1) * S]
                            m = activate(blk, blk, ACT.Silu, scale=vcol(l, V_LG + k), bias=vcol(l, V_LB + k))
                        m.then_inc(s["plain_ready"], 1)
                        round_piece(l, H_CZ, a_hi[:, 1024:2048], cz[:])
                    if CH_CONV <= u < CH_XK[1]:
                        i = u - CH_CONV
                        round_piece(l, H_MIX + i, a_hi[:, i * 1024:(i + 1) * 1024], mixin[:, i * 1024:(i + 1) * 1024])
                    if u == CH_MIX + 3:
                        for i in range(4):
                            round_piece(l, H_H2 + i, a_hi[:, i * 512:(i + 1) * 512], tmp[:, i * 512:(i + 1) * 512])
                    if u == CH_XQ + 1:
                        for h in range(HEADS):
                            act.wait_ge(s["att_max"], l * HEADS + h + 1)
                            for b in range(TB):
                                i = h * TB + b
                                m = activate(probs[:, i * S:(i + 1) * S], M[h][:, b * S:(b + 1) * S], ACT.Exp, scale=SCALE,
                                             bias=neg_max[:, i:i + 1], accum_out=exp_sum[:, i:i + 1])
                            m.then_inc(s["att_exp"], 1)
                    if u == CH_XV[1]:
                        for h in range(HEADS):
                            act.wait_ge(s["att_T"], l * HEADS + h + 1)
                            copy(pT[:, h * 512:(h + 1) * 512], M[h][:]).then_inc(s["att_pT"], 1)
                        for i in range(2):
                            h = slice(i * 512, (i + 1) * 512)
                            act.wait_ge(s["att_o"], l * HEADS + 2 * i + 2)
                            copy(a_hi[:, h], M[i][:]).then_inc(s["part_hi"], 1)

                def round_tokens(n, i):
                    act.wait_ge(s["tok_T"], l * 4 + n + 1)
                    copy(a_hi[:, i * 512:(i + 1) * 512], M[i][:]).then_inc(s["tok_hi"], 1)

                round_tokens(0, 0)
                round_tokens(1, 2)
                act.wait_ge(s["logits"], l + 1)
                activate(scores_T, R[0][:, 0:S], ACT.Sigmoid).then_inc(s["router_sig"], 1)
                round_tokens(2, 1)
                round_tokens(3, 3)
                g0 = act.snap(l + pairs)
                act.sem_inc(s["y_copied"], 4)

                def keep_gathered(i, g, src):
                    act.wait_ge(s["gathered"], g * 4 + i + 1)
                    dst = xg[:].rearrange("p (x k h n) -> p x k h n", x=2, k=KD, h=2)
                    for x in range(2):
                        m = copy(dst[:, x, (i % 2) * 4:(i % 2) * 4 + 4, i // 2, :],
                                 src[:].rearrange("p (k x n) -> p k x n", k=4, x=2)[:, :, x, :])
                    m.then_inc(s["xg_ready"], 1)

                for i in range(4):
                    keep_gathered(i, g0, GATHER_BANKS[i])
                n = iterations(act, l)
                with act.Fori(0, n) as step:
                    for of_step in range(UNROLL):
                        it = act.snap(step * UNROLL + of_step)
                        t = act.snap(pairs + it)
                        g = act.snap(t + l)
                        pair_rounds = act.snap((l + 1) * (DENSE // RAW) + t * (PAIR // RAW))
                        for q in range(PAIR):
                            act.wait_ge(s["expert_used"], t * PAIR + q + 1)
                            if q == 1:
                                copy(gu[:, 0:512], GATE[:]).then_inc(s["gate_copied"], 1)
                            if q in (3, 7):
                                copy(gu[:, 512:1024], UP[:]).then_inc(s["up_copied"], 1)
                            if q == 4:
                                activate(table_out, eps, ACT.Silu).then_inc(s["silu_table"], 1)
                            if q == 6:
                                act.wait_ge(s["gatedT_psum"], t + 1)
                                copy(gatedT, GB[:]).then_inc(s["gatedT_ready"], 1)
                            if q in (9, 11):
                                x = (q - 9) // 2
                                for o in range(2):
                                    copy(ye[:, x * D + o * 512:x * D + (o + 1) * 512], DN[2 * x + o][:]).then_inc(s["y_copied"], 1)
                            round_chunk(q + AHEAD, pair_rounds)
                            if q in (5, 7):
                                x = q // 7
                                if x == 0:
                                    act.wait_ge(s["silu_table"], t + 1)
                                act.wait_ge(s["turned"], t * 2 + x + 1)
                                activate(silu[:, x * S:(x + 1) * S], HT[:, 0:S], ACT.Silu).then_inc(s["he_silu"], 1)
                            if q == 5:
                                copy(gu[:, 0:512], GATE[:]).then_inc(s["gate_copied"], 1)
                            for i in {7: (0,), 8: (1, 2), 9: (3,)}.get(q, ()):
                                keep_gathered(i, g + 1, GATHER_BANKS[i])
                add_pairs(act, pairs_done, n)
                steps_done = act.snap((act.snap(pairs_done) + l) * 4)
                for i in range(4):
                    act.wait_ge(s["added"], steps_done + i + 1)
                    square(i)
                norm_root(act.snap(l + 1), 0, HT)
                round_h(act.snap(l + 1))

        @block.vector
        def _(dve):
            ve = nc.vector

            def links(name, base, per):
                state = [0]

                def link(ins):
                    state[0] += 1
                    ins.then_inc(s[name], 1)
                    dve.wait_ge(s[name], state[0] if base is None else base * per + state[0])

                return link, state

            def rest(out, src, hi):
                return ve.tensor_tensor(out, src, hi.bitcast(F32), ALU.subtract)

            def norm(l, n, col, link, name, first_piece=None):
                dve.wait_ge(s["norm_root"], l * 3 + n + 1)
                link(ve.reciprocal(rstd[:], rstd[:]))
                for i in range(5):
                    if i < 4:
                        for k in (2 * i, 2 * i + 1):
                            m = ve.scalar_tensor_tensor(out=tmp[:, k * S:(k + 1) * S], in0=xT[:, k * S:(k + 1) * S],
                                                        scalar=vcol(l, col + k), in1=rstd[:], op0=ALU.mult, op1=ALU.mult)
                        m.then_inc(s[name], 1)
                    if i and first_piece is not None:
                        h = slice((i - 1) * 512, i * 512)
                        rest_of_piece(l, first_piece + i - 1, a_lo[:, h], tmp[:, h], a_hi[:, h])

            def rest_of_piece(l, i, dst, src, hi):
                dve.wait_ge(s["part_hi"], l * PIECES + i + 1)
                rest(dst, src, hi).then_inc(s["part_split"], 1)

            def first_rest(c):
                dve.wait_ge(s["hi_done"], c + 1)
                rest(part(wlo, c), raw_chunk(c), part(whi, c)).then_inc(s["split_done"], 1)

            link, _ = links("start_link", None, 0)
            dve.wait_ge(s["pos_in"], 32)
            ang, turns, pos = gates[:, 256:512], gates[:, 512:768], gates[:, 768:1024]
            link(ve.tensor_copy(pos, pos_i))
            link(ve.tensor_scalar(ang, pos, glob[:, G_FREQ:G_FREQ + 1], None, ALU.mult))
            link(ve.tensor_scalar(turns, ang, float(1.0 / TWO_PI), MAGIC, ALU.mult, ALU.add))
            link(ve.tensor_scalar(turns, turns, -MAGIC, None, ALU.add))
            for c in (PI_A, PI_B, PI_C):
                link(ve.scalar_tensor_tensor(out=ang, in0=turns, scalar=-c, in1=ang, op0=ALU.mult, op1=ALU.add))
            link(ve.tensor_scalar(ang, ang, 3.1415925, -3.1415925, ALU.min, ALU.max))
            link(ve.tensor_scalar(turns, ang, -1.0, None, ALU.mult))
            link(ve.tensor_tensor(turns, turns, ang, ALU.max))
            ve.tensor_scalar(turns, turns, -1.0, float(np.pi / 2), ALU.mult, ALU.add).then_inc(s["angle"], 1)
            dve.wait_ge(s["x_in"], 16)
            dve.wait_ge(s["const_in"], 32)
            first_rest(0)
            norm(0, 0, V_MIX, link, "plain_ready", H_H)
            for c in range(1, AHEAD):
                first_rest(c)
            dve.wait_ge(s["mem_root"], 1)
            link(ve.reciprocal(rmem[:], rmem[:]))
            pairs_done = counter(dve)
            with dve.Fori(0, depth) as l:
                link, n_links = links("link", l, DVE_LINKS)
                taps_done = 0
                pairs = dve.snap(pairs_done)
                base = dve.snap(l * DENSE + pairs * PAIR)

                def job(j):
                    return R[j % RB]

                def rest_of_chunk(c, chunk_base):
                    dve.wait_ge(s["hi_done"], chunk_base + c + 1)
                    rest(part(wlo, c), raw_chunk(c), part(whi, c)).then_inc(s["split_done"], 1)

                def add_to_x(j):
                    i = j - (JOB[CH_MIX] if j < JOB[CH_XQ] else JOB[CH_XO])
                    q = slice(i * 512, (i + 1) * 512)
                    ve.tensor_tensor(xT[:, q], xT[:, q], job(j)[:], ALU.add).then_inc(bank_free[j % RB], 1)

                for c in range(AHEAD, DENSE + AHEAD):
                    u = c - AHEAD
                    dve.wait_ge(s["proj_done"], l * JOBS + JOB[u + 1])
                    if u == 0:
                        ve.memset(zp[:].rearrange("p (c z) -> p c z", c=CB)[:, :, 0:TAPS - 1], 0.0)
                        dve.wait_ge(s["mem_in"], (l + 1) * 16)
                    if u < 2:
                        for k in range(4 * u, 4 * u + 4):
                            m = ve.scalar_tensor_tensor(out=qk[:, k * S:(k + 1) * S], in0=qk[:, k * S:(k + 1) * S],
                                                        scalar=vcol(l, V_MEM + k), in1=rmem[:], op0=ALU.mult, op1=ALU.mult)
                        m.then_inc(s["plain_ready"], 1)
                    if u in (2, 3):
                        h = slice((u - 2) * 1024, (u - 1) * 1024)
                        rest_of_piece(l, H_MEMN + u - 2, b_lo[:, h], qk[:, h], b_hi[:, h])
                    if CH_CA <= u < CH_Q:
                        i = u - CH_CA
                        freed(dve, l, JOB[CH_CG] + i)
                        for k in range(2):
                            b = 2 * i + k
                            m = ve.tensor_tensor(zp[:, b * ZW + TAPS - 1:(b + 1) * ZW], job(JOB[u])[:, k * S:(k + 1) * S],
                                                 sg[:, b * S:(b + 1) * S], ALU.mult)
                        m.then_inc(s["z_made"], 1)
                        dve.wait_ge(s["z_made"], l * 2 + i + 1)
                        dve.sem_inc(bank_free[JOB[u] % RB], 1)
                    if 7 <= u <= 10:
                        i = u - 7
                        dve.wait_ge(s["sin_done"], 1)
                        dve.wait_ge(s["swapped"], l * 4 + i + 1)
                        x = qk[:, i * 512:(i + 1) * 512].rearrange("p (h t) -> p h t", h=2)
                        y = tmp[:, i * 512:(i + 1) * 512].rearrange("p (h t) -> p h t", h=2)
                        two = [P, 2, S]
                        ve.tensor_tensor(y, M[i][:].rearrange("p (h t) -> p h t", h=2), sin[:].unsqueeze(1).broadcast_to(two),
                                         ALU.mult)
                        link(ve.tensor_tensor(x, x, cos[:].unsqueeze(1).broadcast_to(two), ALU.mult))
                        ve.tensor_tensor(x, x, y, ALU.add).then_inc(s["rotated"], 1)
                    if u == 13:
                        dve.wait_ge(s["decay_in"], 16)
                        for h in range(HEADS):
                            dve.wait_ge(s["scores"], l * HEADS + h + 1)
                            decay = const[:, C_DECAY + h * S:C_DECAY + (h + 1) * S]
                            ve.tensor_tensor(sT[:, h * 384:h * 384 + S], M[h][:, 0:S], decay, ALU.mult)
                            ve.tensor_tensor(sT[:, h * 384 + S:h * 384 + 384], M[h][:, S:S + P], decay[:, 0:P], ALU.mult
                                             ).then_inc(s["masked"], 1)
                    if u == 17:
                        dve.wait_ge(s["r_root"], l + 1)
                        ve.reciprocal(r_rms, r_rms).then_inc(s["r_inverse"], 1)
                    if u == 18:
                        dve.wait_ge(s["ln_mean"], l + 1)
                        for k in range(CB):
                            blk = cz[:, k * S:(k + 1) * S]
                            m = ve.scalar_tensor_tensor(out=blk, in0=M[0][:, 0:S], scalar=-1.0 / (CB * P), in1=blk,
                                                        op0=ALU.mult, op1=ALU.add)
                        m.then_inc(s["ln_centred"], 1)
                        dve.wait_ge(s["r_factor"], l + 1)
                        for h in range(HEADS):
                            head = r[:, h * S:(h + 1) * S]
                            m = ve.scalar_tensor_tensor(out=head, in0=head, scalar=vcol(l, V_RET + h),
                                                        in1=M[2 + h // 2][:, (h % 2) * S:(h % 2 + 1) * S], op0=ALU.mult, op1=ALU.mult)
                        link(m)
                        for i in range(2):
                            freed(dve, l, JOB[CH_SG] + i)
                        ve.tensor_tensor(r[:], r[:], sg[:], ALU.mult).then_inc(s["plain_ready"], 1)
                    if u == 20:
                        dve.wait_ge(s["ln_root"], l + 1)
                        link(ve.reciprocal(rstd[:], rstd[:]))
                        z3 = cz[:].rearrange("p (k t) -> p k t", k=CB)
                        ve.tensor_tensor(z3, z3, rstd[:].unsqueeze(1).broadcast_to([P, CB, S]), ALU.mult).then_inc(s["ln_scaled"], 1)
                    if CH_RET <= u < CH_CONV:
                        for i in range(2):
                            j = JOB[u] + i
                            q = slice((j - JOB[CH_RET]) * 512, (j - JOB[CH_RET] + 1) * 512)
                            ve.tensor_tensor(mixin[:, q], job(j)[:], gates[:, q], ALU.mult).then_inc(bank_free[j % RB], 1)
                    if CH_CONV <= u < CH_XK[1]:
                        for i in range(2):
                            j = JOB[u] + i
                            n = j - JOB[CH_CONV]
                            q = slice(n * 512, (n + 1) * 512)
                            ve.tensor_tensor(tmp[:, q], job(j)[:], gates[:, 2048 + n * 512:2048 + (n + 1) * 512], ALU.mult
                                             ).then_inc(bank_free[j % RB], 1)
                            freed(dve, l, j)
                            m = ve.tensor_tensor(mixin[:, q], mixin[:, q], tmp[:, q], ALU.add)
                        m.then_inc(s["plain_ready"], 1)
                    if CH_MIX <= u < CH_MIX + 4:
                        add_to_x(JOB[u])
                    if u >= CH_XO:
                        add_to_x(JOB[u])
                        add_to_x(JOB[u] + 1)
                    if u == CH_MIX + 3:
                        norm(l, 1, V_XATTN, link, "plain_ready", H_H2)
                    if u == DENSE - 1:
                        norm(l, 2, V_FFN, link, "normed")
                    rest_of_chunk(c, base)
                    if u == 19:
                        rest_of_piece(l, H_R, a_lo[:, 0:1024], r[:], a_hi[:, 0:1024])
                    if u == 20:
                        rest_of_piece(l, H_CZ, a_lo[:, 1024:2048], cz[:], a_hi[:, 1024:2048])
                    if CH_CA <= u < CH_CA + len(TAP_STEPS):
                        for n in range(taps_done, min(taps_done + TAP_STEPS[u - CH_CA], TAPS * CB)):
                            w, k = TAP_ORDER[n]
                            src = zp[:, k * ZW + w:k * ZW + w + S]
                            acc = cz[:, k * S:(k + 1) * S]
                            if w == 0:
                                m = ve.tensor_scalar(acc, src, vcol(l, V_TAP + k), vcol(l, V_CB + k), ALU.mult, ALU.add)
                            else:
                                dve.wait_ge(s["conv_tap"], l * (TAPS * CB) + n - 1)
                                m = ve.scalar_tensor_tensor(out=acc, in0=src, scalar=vcol(l, V_TAP + w * CB + k), in1=acc,
                                                            op0=ALU.mult, op1=ALU.add)
                            m.then_inc(s["conv_tap"], 1)
                        taps_done += TAP_STEPS[u - CH_CA]
                    if CH_CONV <= u < CH_XK[1]:
                        i = u - CH_CONV
                        h = slice(i * 1024, (i + 1) * 1024)
                        rest_of_piece(l, H_MIX + i, a_lo[:, h], mixin[:, h], a_hi[:, h])
                    if u == CH_XQ + 1:
                        for h in range(HEADS):
                            dve.wait_ge(s["att_scores"], l * HEADS + h + 1)
                            cols = neg_max[:, h * TB:(h + 1) * TB]
                            link(ve.tensor_reduce(cols, M[h][:].rearrange("p (b m) -> p b m", b=TB), AX, ALU.max))
                            ve.tensor_scalar(cols, cols, -SCALE, None, ALU.mult).then_inc(s["att_max"], 1)
                        for h in range(HEADS):
                            dve.wait_ge(s["att_exp"], l * HEADS + h + 1)
                            cols = exp_sum[:, h * TB:(h + 1) * TB]
                            link(ve.reciprocal(cols, cols))
                            for b in range(TB):
                                i = h * TB + b
                                row = probs[:, i * S:(i + 1) * S]
                                m = ve.tensor_scalar(row, row, exp_sum[:, i:i + 1], None, ALU.mult)
                            m.then_inc(s["att_probs"], 1)
                    if u == CH_XV[1]:
                        for i in range(2):
                            h = slice(i * 512, (i + 1) * 512)
                            rest_of_piece(l, H_O + i, a_lo[:, h], M[i][:], a_hi[:, h])
                        ve.memset(ye, 0.0)
                        ve.memset(gatedT, 0.0).then_inc(s["zeroed"], 1)

                def rest_of_tokens(n, i):
                    dve.wait_ge(s["tok_hi"], l * 4 + n + 1)
                    q = slice(i * 512, (i + 1) * 512)
                    rest(a_lo[:, q], M[i][:], a_hi[:, q]).then_inc(s["tok_split"], 1)

                rest_of_tokens(0, 0)
                rest_of_tokens(1, 2)
                dve.wait_ge(s["score_turned"], l + 1)
                by16, by4 = [P, TB, E], [P, TB, 4]
                sel3, keyed3, ch3, hot3, gate3 = (a.rearrange("p (b e) -> p b e", b=TB)
                                                          for a in (sel, keyed, chosen, hot2, gate))
                group3, in3 = (a.rearrange("p (b g) -> p b g", b=TB) for a in (group, ingroup))
                key4 = const[:, C_KEY4:C_KEY4 + 4].unsqueeze(1).broadcast_to(by4)
                key16 = const[:, C_KEY16:C_KEY16 + E].unsqueeze(1).broadcast_to(by16)
                link(ve.tensor_tensor(sel3, score3, glob[:, G_BR:G_BR + E].unsqueeze(1).broadcast_to(by16), ALU.add))
                s4 = sel.rearrange("p (g m) -> p g m", m=4)
                p4 = keyed.rearrange("p (g m) -> p g m", m=4)
                ve.tensor_tensor(p4[:, :, 0:3], s4[:, :, 0:3], s4[:, :, 1:4], ALU.add)
                ve.tensor_tensor(sums.rearrange("p (g m) -> p g m", m=4)[:, :, 0:2], s4[:, :, 0:2], s4[:, :, 2:4], ALU.add)
                link(ve.tensor_tensor(p4[:, :, 3:4], s4[:, :, 0:1], s4[:, :, 3:4], ALU.add))
                link(ve.tensor_tensor(p4[:, :, 0:2], p4[:, :, 0:2], sums.rearrange("p (g m) -> p g m", m=4)[:, :, 0:2], ALU.max))
                link(ve.tensor_reduce(group, p4, AX, ALU.max))

                def first_best(values, keys, shape, hot, scratch):
                    spread = best.unsqueeze(2).broadcast_to(shape)
                    link(ve.tensor_reduce(best, values, AX, ALU.max))
                    link(ve.tensor_tensor(scratch, values, spread, ALU.is_equal))
                    link(ve.tensor_tensor(scratch, scratch, keys, ALU.mult))
                    link(ve.tensor_reduce(best, scratch, AX, ALU.max))
                    link(ve.tensor_tensor(hot, keys, spread, ALU.is_equal))

                first_best(group3, key4, by4, in3, sums[:, 0:8].rearrange("p (b g) -> p b g", b=TB))
                link(ve.tensor_scalar(ingroup, ingroup, BIG, -BIG, ALU.mult, ALU.add))
                link(ve.tensor_tensor(s4, s4, ingroup.unsqueeze(2).broadcast_to([P, TB * 4, 4]), ALU.add))
                first_best(sel3, key16, by16, ch3, keyed3)
                link(ve.scalar_tensor_tensor(out=sel, in0=chosen, scalar=-BIG, in1=sel, op0=ALU.mult, op1=ALU.add))
                first_best(sel3, key16, by16, hot3, keyed3)
                ve.tensor_tensor(chosen, chosen, hot2, ALU.add).then_inc(s["chosen"], 1)
                dve.wait_ge(s["chosen"], l + 1)
                link(ve.tensor_tensor(sel3, score3, ch3, ALU.mult))
                link(ve.tensor_reduce(best, sel3, AX, ALU.add))
                link(ve.reciprocal(best, best))
                ve.tensor_tensor(gate3, sel3, best.unsqueeze(2).broadcast_to(by16), ALU.mult)
                dve.wait_ge(s["ranks"], l + 1)
                link(ve.scalar_tensor_tensor(out=place, in0=R[1][:, 0:2 * E], scalar=1.0, in1=chosen, op0=ALU.add, op1=ALU.mult))
                def make_onehot(it, twice=False):
                    pair = dve.snap(it % PAIRS)
                    slots = const[:, bass.ds(dve.snap(it // PAIRS * P) + C_IOTA, P if twice else SLOTS)]
                    for b in range(TB):
                        for x in range(2):
                            mine = place[:, bass.ds(pair * 2 + (b * E + x), 1)]
                            if twice:
                                share = gate[:, bass.ds(pair * 2 + (b * E + x), 1)]
                                n = (b * 2 + x) * P
                                m = ve.tensor_scalar(gated[:, n:n + P], slots, mine, share, ALU.is_equal, ALU.mult)
                            else:
                                n = b * P + x * SLOTS
                                m = ve.tensor_scalar(onehot[:, n:n + SLOTS], slots, mine, None, ALU.is_equal)
                    m.then_inc(s["gated_ready" if twice else "onehot_ready"], 1)

                slots = const[:, C_IOTA:C_IOTA + SLOTS]
                for b in range(TB):
                    for x in range(2):
                        n = b * P + x * SLOTS
                        m = ve.tensor_scalar(onehot[:, n:n + SLOTS], slots, place[:, b * E + x:b * E + x + 1], None, ALU.is_equal)
                m.then_inc(s["onehot_ready"], 1)
                rest_of_tokens(2, 1)
                link(ve.tensor_reduce(best[:, 0:1], R[1][:, 2 * E:3 * E], AX, ALU.max))
                steps = const[0:1, C_IOTA + P:C_IOTA + 4 * P].rearrange("p (n m) -> p n m", m=P)[:, :, 0]
                link(ve.tensor_scalar(keyed[0:1, 0:3], steps, best[0:1, 0:1], None, ALU.is_le))
                link(ve.tensor_reduce(best[0:1, 0:1], keyed[0:1, 0:3], AX, ALU.add))
                ve.tensor_scalar(count[0:1, 0:1], best[0:1, 0:1], float(STEPS), float(STEPS), ALU.mult, ALU.add
                                 ).then_inc(s["sweeps_known"], 1)
                rest_of_tokens(3, 3)
                n = iterations(dve, l)
                with dve.Fori(0, n) as step:
                    for of_step in range(UNROLL):
                        it = dve.snap(step * UNROLL + of_step)
                        t = dve.snap(pairs + it)
                        g = dve.snap(t + l)
                        pair_base = dve.snap(t * PAIR + (l + 1) * DENSE)

                        def hidden(x):
                            h = he[:, x * S:(x + 1) * S]
                            h4 = h.rearrange("p (f n) -> p f n", f=4)
                            parts = he_parts[:, x * 512:(x + 1) * 512].rearrange("p (f h n) -> p f h n", f=4, h=2)
                            dve.wait_ge(s["he_silu"], t * 2 + x + 1)
                            ve.tensor_tensor(h, silu[:, x * S:(x + 1) * S], HT[:, S:2 * S], ALU.mult).then_inc(s["pair_link"], 1)
                            dve.wait_ge(s["pair_link"], t * 4 + 2 * x + 1)
                            ve.tensor_copy(parts[:, :, 0, :], h4).then_inc(s["pair_link"], 1)
                            dve.wait_ge(s["pair_link"], t * 4 + 2 * x + 2)
                            rest(parts[:, :, 1, :], h4, parts[:, :, 0, :]).then_inc(s["he_split"], 1)

                        for q in range(PAIR):
                            dve.wait_ge(s["expert_used"], t * PAIR + q + 1)
                            if q == 3:
                                make_onehot(dve.snap(it + 1))
                            if q == 5:
                                hidden(0)
                            rest_of_chunk(q + AHEAD, pair_base)
                            if q == 7:
                                hidden(1)
                            if q == 2:
                                make_onehot(it, twice=True)
                            if 1 <= q <= 4:
                                i = q - 1
                                x4 = slice(i * 512, (i + 1) * 512)
                                dve.wait_ge(s["scattered"], g * 4 + i + 1)
                                ve.tensor_tensor(xT[:, x4], xT[:, x4], DN[i][:], ALU.add).then_inc(s["added"], 1)
                add_pairs(dve, pairs_done, n)
                steps_done = dve.snap((dve.snap(pairs_done) + l) * 4)
                for i in range(4):
                    x4 = slice(i * 512, (i + 1) * 512)
                    dve.wait_ge(s["scattered"], steps_done + i + 1)
                    ve.tensor_tensor(xT[:, x4], xT[:, x4], DN[i][:], ALU.add).then_inc(s["added"], 1)
                norm(dve.snap(l + 1), 0, V_MIX, link, "plain_ready", H_H)
                assert n_links[0] == DVE_LINKS, ("DVE_LINKS", n_links[0])


def constants():
    c = np.zeros((P, C_ALL), np.float32)
    i = np.arange(P)
    c[i, C_ID + i] = 1
    c[:, C_ONE:C_ONE + P] = 1
    half = P // 2
    c[np.arange(half) + half, C_SWAP + np.arange(half)] = -1
    c[np.arange(half), C_SWAP + half + np.arange(half)] = 1
    c[:, C_BEFORE:C_BEFORE + P] = i[:, None] < i[None, :]
    gap = np.arange(S)[None, :] - i[:, None]
    for h in range(HEADS):
        log_gamma = np.log(1.0 - 2.0 ** (-5.0 - h))
        c[:, C_DECAY + h * S:C_DECAY + (h + 1) * S] = np.where(gap >= 0, np.exp(np.maximum(gap, 0) * log_gamma) * SCALE, 0.0)
    for n in range(S // SLOTS + 1):
        c[:, C_IOTA + n * P:C_IOTA + (n + 1) * P] = n * SLOTS + i % SLOTS + 1
    c[:, C_BAND + 3 * 32:C_BAND + 4 * 32] = 1
    c[:, C_EPS] = EPS
    c[i, C_BOTH + i % SLOTS] = 1
    c[:, C_KEY4:C_KEY4 + 4] = 4 - np.arange(4)
    c[:, C_KEY16:C_KEY16 + E] = E - np.arange(E)
    return c


def columns(a):
    a = np.asarray(a)
    return np.moveaxis(a.reshape(*a.shape[:-1], -1, P), -1, 0)


def blocks(w, cols):
    rows = w.shape[0]
    return w.reshape(rows // P, P, -1, cols).transpose(2, 1, 0, 3).reshape(-1, P, rows // P * cols)


def chunks(w, cols):
    return blocks(np.asarray(w), cols)


def kernel(x, mem, positions, norm_mix_g, w_in, b_branch_gate, ret_norm_g, w_ret_out, conv_w, conv_b, conv_ln_g,
           conv_ln_b, w_conv_out, w_mix_out, norm_xattn_g, norm_mem_g, w_xq, w_xkv, w_xo, norm_ffn_g, w_router,
           b_router, w_exp_gate, w_exp_up, w_exp_down, norm_final_g):
    import concourse.bacc as bacc
    from concourse.bass_utils import run_bass_kernel_spmd

    depth = w_in.shape[0]
    vec = np.zeros((P, depth + 1, V_ALL), np.float32)
    for at, a in ((V_MIX, norm_mix_g), (V_XATTN, norm_xattn_g), (V_MEM, norm_mem_g), (V_FFN, norm_ffn_g),
                  (V_BG, b_branch_gate), (V_RET, ret_norm_g), (V_CB, conv_b), (V_LG, conv_ln_g), (V_LB, conv_ln_b)):
        a = columns(a)
        vec[:, :depth, at:at + a.shape[2]] = a
    vec[:, depth, V_MIX:V_MIX + KD] = columns(norm_final_g)
    vec[:, :depth, V_TAP:] = columns(conv_w).reshape(P, depth, TAPS * CB)
    glob = np.zeros((P, G_ALL), np.float32)
    glob[:, G_RT:G_RT + KD * E] = np.asarray(w_router).reshape(KD, P, E).transpose(1, 0, 2).reshape(P, -1)
    glob[:, G_BR:G_BR + E] = np.asarray(b_router)[None, :]
    glob[:, G_FREQ] = np.float32(10000.0) ** (-(np.arange(P) % (P // 2)).astype(np.float32) / (P // 2))
    dense = np.empty((depth, DENSE, P, CHUNK), np.float32)
    experts = np.empty((depth * PAIRS, PAIR, P, CHUNK), np.float32)
    for l in range(depth):
        win = chunks(w_in[l], 256).reshape(10, 2, P, CHUNK)
        for at, n, m in ((CH_Q, 0, 1), (CH_K, 1, 1), (CH_V, 2, 1), (CH_SG, 3, 1), (CH_CA, 4, 1), (CH_CG, 5, 1), (CH_G, 6, 4)):
            dense[l, at:at + 2 * m] = win[n:n + m].reshape(-1, P, CHUNK)
        xkv = chunks(w_xkv[l], 256)
        for at, w in ((CH_RET, chunks(w_ret_out[l], 512)), (CH_CONV, chunks(w_conv_out[l], 512)), (CH_MIX, chunks(w_mix_out[l], 256)),
                      (CH_XQ, chunks(w_xq[l], 256)), (CH_XO, chunks(w_xo[l], 512))):
            dense[l, at:at + len(w)] = w
        for at, w in zip(CH_XK + CH_XV, xkv):
            dense[l, at] = w
        for e in range(E):
            pair, second = l * PAIRS + e // 2, e % 2
            for at, w, cols in ((4 * second, w_exp_gate, 512), (4 * second + 2, w_exp_up, 512),
                                (8 + 2 * second, w_exp_down, D)):
                unit = chunks(w[l, e], cols)[0]
                experts[pair, at], experts[pair, at + 1] = unit[:, :CHUNK], unit[:, CHUNK:]

    def turned(a):
        return np.ascontiguousarray(np.asarray(a)[0].T.reshape(KD, P, S).transpose(1, 0, 2))

    arrays = {
        "x_in": turned(x), "mem_in": turned(mem),
        "positions_in": np.ascontiguousarray(np.broadcast_to(np.asarray(positions)[None, :], (P, S))),
        "constants_in": constants(), "vectors_in": vec.reshape(P, -1), "globals_in": glob,
        "dense_in": dense, "experts_in": experts,
    }
    nc = bacc.Bacc("TRN2", target_bir_lowering=False, num_devices=1)
    args = [nc.dram_tensor(n, a.shape, mybir.dt.from_np(a.dtype), kind="ExternalInput").ap() for n, a in arrays.items()]
    out = nc.dram_tensor("out", (P, KD, S), F32, kind="ExternalOutput").ap()
    build(nc, *args, out)
    got = run_bass_kernel_spmd(nc, [arrays], core_ids=[0]).results[0]["out"]
    return np.ascontiguousarray(got.transpose(2, 1, 0).reshape(1, S, D))
```
